# Optimizing a Trainium2 kernel written in Bass

```python
import jax, jax.numpy as jnp
from jax import lax
import numpy as np

D_MODEL = 1024
BATCH = 1
SEQ = 1024
DEPTH = 1

CHUNK = 64
Q_BLOCK = 2 * CHUNK
D_MIX = D_MODEL
ATTN_HEADS = 8
HEAD_DIM = 64
D_ATTN = ATTN_HEADS * HEAD_DIM
D_CONV = D_MIX - D_ATTN
CONV_WIDTH = 3
N_EXPERTS = 32
TOP_K = 4
D_EXPERT = D_MODEL
SWIGLU_LIMIT = 7.0
SWIGLU_ALPHA = 1.702
MOE_BLOCK = 128
N_MOD = 6
EPS = 1e-6
SPLITS = (D_ATTN, 2 * D_ATTN, 3 * D_ATTN, 3 * D_ATTN + ATTN_HEADS,
          3 * D_ATTN + ATTN_HEADS + D_CONV, 3 * D_ATTN + ATTN_HEADS + 2 * D_CONV)
D_IN_PROJ = 3 * D_ATTN + ATTN_HEADS + 3 * D_CONV

kernel_name = "hybrid_fox_shortconv_moe_adaln"

def rms_norm(x, w):
    xf = x.astype(jnp.float32)
    y = xf * lax.rsqrt(jnp.mean(xf * xf, axis=-1, keepdims=True) + EPS)
    return (y * w.astype(jnp.float32)).astype(x.dtype)

def forgetting_attention(q, k, v, log_f):
    s_len = q.shape[2]
    cum = jnp.cumsum(log_f, axis=-1)
    scale = HEAD_DIM ** -0.5
    outs = []
    for i in range(s_len // Q_BLOCK):
        q0, q1 = i * Q_BLOCK, (i + 1) * Q_BLOCK
        s = jnp.einsum('bhqd,bhkd->bhqk', q[:, :, q0:q1], k[:, :, :q1],
                       preferred_element_type=jnp.float32) * scale
        s = s + cum[:, :, q0:q1, None] - cum[:, :, None, :q1]
        q_pos = q0 + jnp.arange(Q_BLOCK)
        k_pos = jnp.arange(q1)
        s = jnp.where(k_pos[None, :] <= q_pos[:, None], s, -jnp.inf)
        p = jax.nn.softmax(s, axis=-1)
        outs.append(jnp.einsum('bhqk,bhkd->bhqd', p.astype(v.dtype), v[:, :, :q1]))
    return jnp.concatenate(outs, axis=2)

def causal_short_conv(u, w):
    s_len = u.shape[1]
    up = jnp.pad(u, ((0, 0), (CONV_WIDTH - 1, 0), (0, 0)))
    y = w[0] * up[:, 0:s_len]
    for j in range(1, CONV_WIDTH):
        y = y + w[j] * up[:, j:j + s_len]
    return y

def moe_ffn(h, w_router, b_router, w_gate_up, b_gate_up, w_down, b_down):
    bsz, s_len, d = h.shape
    t = bsz * s_len
    hf = h.reshape(t, d)
    logits = jnp.einsum('td,de->te', hf, w_router, preferred_element_type=jnp.float32) \
        + b_router.astype(jnp.float32)
    top_logits, top_idx = lax.top_k(logits, TOP_K)
    top_w = jax.nn.softmax(top_logits, axis=-1)
    n_assign = t * TOP_K
    flat_e = top_idx.reshape(n_assign)
    order = jnp.argsort(flat_e)
    sorted_e = flat_e[order]
    sorted_tok = (order // TOP_K).astype(jnp.int32)
    sorted_w = top_w.reshape(n_assign)[order]
    counts = jnp.bincount(flat_e, length=N_EXPERTS)
    padded = (counts + MOE_BLOCK - 1) // MOE_BLOCK * MOE_BLOCK
    pad_end = jnp.cumsum(padded)
    pad_start = pad_end - padded
    start = jnp.cumsum(counts) - counts
    dest = pad_start[sorted_e] + (jnp.arange(n_assign) - start[sorted_e])
    n_blocks = -(-n_assign // MOE_BLOCK) + N_EXPERTS
    n_rows = n_blocks * MOE_BLOCK
    row_tok = jnp.zeros((n_rows,), jnp.int32).at[dest].set(sorted_tok)
    row_w = jnp.zeros((n_rows,), jnp.float32).at[dest].set(sorted_w)
    block_e = jnp.minimum(
        jnp.searchsorted(pad_end, jnp.arange(n_blocks) * MOE_BLOCK, side='right'), N_EXPERTS - 1)
    xb = hf[row_tok].reshape(n_blocks, MOE_BLOCK, d)

    def expert_block(args):
        xe, e = args
        gu = xe @ w_gate_up[e] + b_gate_up[e]
        gate, up = jnp.split(gu, 2, axis=-1)
        gate = jnp.minimum(gate, SWIGLU_LIMIT)
        up = jnp.clip(up, -SWIGLU_LIMIT, SWIGLU_LIMIT)
        act = gate * jax.nn.sigmoid(SWIGLU_ALPHA * gate) * (up + 1)
        return act @ w_down[e] + b_down[e]

    yb = lax.map(expert_block, (xb, block_e))
    y_rows = yb.reshape(n_rows, d) * row_w[:, None].astype(yb.dtype)
    return jnp.zeros_like(hf).at[row_tok].add(y_rows).reshape(bsz, s_len, d)

def setup_inputs(seed: int = 0) -> dict:
    key = jax.random.key(seed)
    ks = jax.random.split(key, 20)
    L, D = DEPTH, D_MODEL
    nrm = jax.random.normal
    return {
        "x": nrm(ks[0], (BATCH, SEQ, D), jnp.float32),
        "c": nrm(ks[1], (BATCH, D), jnp.float32),
        "w_ada": nrm(ks[2], (L, D, N_MOD * D), jnp.float32) * (0.5 * D ** -0.5),
        "b_ada": nrm(ks[3], (L, N_MOD * D), jnp.float32) * 0.01,
        "norm1_w": 1.0 + 0.1 * nrm(ks[4], (L, D), jnp.float32),
        "w_in": nrm(ks[5], (L, D, D_IN_PROJ), jnp.float32) * D ** -0.5,
        "b_forget": 3.0 + 0.5 * nrm(ks[6], (L, ATTN_HEADS), jnp.float32),
        "q_norm_w": 1.0 + 0.1 * nrm(ks[7], (L, HEAD_DIM), jnp.float32),
        "k_norm_w": 1.0 + 0.1 * nrm(ks[8], (L, HEAD_DIM), jnp.float32),
        "conv_w": nrm(ks[9], (L, CONV_WIDTH, D_CONV), jnp.float32) * CONV_WIDTH ** -0.5,
        "attn_out_norm_w": 1.0 + 0.1 * nrm(ks[10], (L, D_ATTN), jnp.float32),
        "conv_out_norm_w": 1.0 + 0.1 * nrm(ks[11], (L, D_CONV), jnp.float32),
        "w_out": nrm(ks[12], (L, D_MIX, D), jnp.float32) * D_MIX ** -0.5,
        "norm2_w": 1.0 + 0.1 * nrm(ks[13], (L, D), jnp.float32),
        "w_router": nrm(ks[14], (L, D, N_EXPERTS), jnp.float32) * D ** -0.5,
        "b_router": nrm(ks[15], (L, N_EXPERTS), jnp.float32) * 0.01,
        "w_gate_up": nrm(ks[16], (L, N_EXPERTS, D, 2 * D_EXPERT), jnp.float32) * D ** -0.5,
        "b_gate_up": nrm(ks[17], (L, N_EXPERTS, 2 * D_EXPERT), jnp.float32) * 0.01,
        "w_down": nrm(ks[18], (L, N_EXPERTS, D_EXPERT, D), jnp.float32) * D_EXPERT ** -0.5,
        "b_down": nrm(ks[19], (L, N_EXPERTS, D), jnp.float32) * 0.01,
    }

def reference(x, c, w_ada, b_ada, norm1_w, w_in, b_forget, q_norm_w, k_norm_w, conv_w,
              attn_out_norm_w, conv_out_norm_w, w_out, norm2_w, w_router, b_router,
              w_gate_up, b_gate_up, w_down, b_down):
    bsz, s_len, _ = x.shape

    def to_heads(t):
        return t.reshape(bsz, s_len, ATTN_HEADS, HEAD_DIM).transpose(0, 2, 1, 3)

    for l in range(DEPTH):
        mod = jnp.einsum('bd,de->be', jax.nn.silu(c), w_ada[l]) + b_ada[l]
        sh1, sc1, g1, sh2, sc2, g2 = jnp.split(mod[:, None, :], N_MOD, axis=-1)

        h = rms_norm(x, norm1_w[l]) * (1 + sc1) + sh1
        proj = h @ w_in[l]
        q, k, v, f_logit, gb, gc, u = jnp.split(proj, SPLITS, axis=-1)

        qh = rms_norm(to_heads(q), q_norm_w[l])
        kh = rms_norm(to_heads(k), k_norm_w[l])
        vh = to_heads(v)
        log_f = jax.nn.log_sigmoid((f_logit + b_forget[l]).astype(jnp.float32)).transpose(0, 2, 1)
        attn = forgetting_attention(qh, kh, vh, log_f)
        attn = attn.transpose(0, 2, 1, 3).reshape(bsz, s_len, D_ATTN)

        conv = gb * causal_short_conv(gc * u, conv_w[l])

        mixed = jnp.concatenate([rms_norm(attn, attn_out_norm_w[l]),
                                 rms_norm(conv, conv_out_norm_w[l])], axis=-1)
        x = x + g1 * (mixed @ w_out[l])

        h2 = rms_norm(x, norm2_w[l]) * (1 + sc2) + sh2
        x = x + g2 * moe_ffn(h2, w_router[l], b_router[l], w_gate_up[l], b_gate_up[l],
                             w_down[l], b_down[l])
    return x


_drawn_inputs = setup_inputs


def setup_inputs(seed=0):
    import zlib

    import numpy as np

    out = dict(_drawn_inputs(seed))
    spreads = {}
    factors = {'b_ada': 3.027,
     'q_norm_w': 3.563,
     'k_norm_w': 3.945,
     'b_router': 6.101,
     'b_gate_up': 29.273,
     'b_down': 35.677}
    for name, (base, spread) in spreads.items():
        noise = np.random.default_rng([zlib.crc32(name.encode()), seed]).standard_normal(out[name].shape)
        drawn = base * np.exp(spread * noise) if base else spread * noise
        out[name] = __import__('jax').numpy.asarray(drawn.astype(out[name].dtype))
    for name, factor in factors.items():
        out[name] = (out[name] * factor).astype(out[name].dtype)
    return out
```

```python
from contextlib import ExitStack

import concourse.bass as bass
from concourse import mybir

ALU = mybir.AluOpType
ACT = mybir.ActivationFunctionType
AX_X = mybir.AxisListType.X
F32 = mybir.dt.float32
F32R = mybir.dt.float32r
BF16 = mybir.dt.bfloat16
I32 = mybir.dt.int32
U32 = mybir.dt.uint32

P = 128
EPS = 1e-6
NEG = -(2.0 ** 100)


class Chain:

    def __init__(self, eng, sem, start=0):
        self.eng, self.sem, self.start, self.n = eng, sem, start, 0

    def link(self, ins):
        ins.then_inc(self.sem, 1)
        self.n += 1
        self.eng.wait_ge(self.sem, self.start + self.n)


class Shared:

    def semaphores(self, nc):
        self.held = []

        def sem(name):
            self.held.append(nc.alloc_semaphore(name=name))
            return self.held[-1]

        self.idle = sem(f"idle{nc.next_id()}")
        return sem

    def settle(self, eng):
        eng.sem_inc(self.idle, 1)

    def release(self, nc):
        nc.clear_and_free_semaphores(self.held)
        nc.all_engine_barrier()


def shared(nc, ctx, a):
    s = Shared()
    s.T, s.D = a["x"].shape[1], a["x"].shape[2]
    s.NT, s.KT = s.T // P, s.D // P
    s.H, s.HD = a["b_forget"].shape[1], a["q_norm_w"].shape[1]
    s.DA, s.DC = s.H * s.HD, a["conv_w"].shape[2]
    s.CT = s.DC // P
    s.E, s.TOPK = a["w_gate_up"].shape[1], 4
    s.GB = 256
    s.HALF = 512
    assert s.T == s.D == 1024 and s.DA == s.DC == 512 and s.HD == 64 and s.E == 32

    def sb(name, shape, dt, stack=ctx):
        return stack.enter_context(nc.sbuf_tensor(name, shape, dt))

    s.sb = sb
    dram = lambda name, shape, dt: nc.dram_tensor(name, shape, dt).ap()
    s.qT_d = dram("qT_d", [s.DA, s.T], F32)
    s.kT_d = dram("kT_d", [s.DA, s.T], F32)
    s.v_d = dram("v_d", [s.T, s.DA], F32)
    s.extq_d = dram("extq_d", [s.H, 4, s.T], F32)
    s.extk_d = dram("extk_d", [s.H, 4, s.T], F32)
    s.x1_d = dram("x1_d", [s.T, s.D], F32)
    s.xn_d = dram("xn_d", [s.T, s.D], F32)
    s.list_d = dram("list_d", [s.E * s.T, 2], I32)
    s.y_d = dram("y_d", [s.T * s.TOPK + P, s.D], F32)

    s.ident = sb("ident", [P, P], F32)
    s.eps = sb("eps", [P, 1], F32)
    s.ones_row = sb("ones_row", [1, P], F32)
    s.csilu = sb("csilu", [P, s.KT], F32)
    s.shift2 = sb("shift2", [P, s.KT], F32)
    s.gain2 = sb("gain2", [P, s.KT], F32)
    s.topw_all = sb("topw_all", [P, s.NT, s.TOPK], F32)
    s.table = sb("table", [1, 2, s.E + 1], I32)
    s.gate2 = sb("gate2", [P, s.D], F32)
    s.mask = sb("mask", [P, P], F32R)
    s.ident_r = sb("ident_r", [P, P], F32R)
    s.psum = ctx.enter_context(nc.psum_tensor("psum", [P, 8, 512], F32))
    return s


def project_block(nc, s, a):
    T, D, NT, KT, CT, H, HALF = s.T, s.D, s.NT, s.KT, s.CT, s.H, s.HALF
    SW = 256
    PIECE = 2
    NP = KT // PIECE
    psum = s.psum
    DA, DC = s.DA, s.DC
    NADA = 2 * D // SW
    f0 = 3 * DA
    g0 = f0 + H
    slabs = []
    for base, kind in ((0, "q"), (DA, "k")):
        slabs += [(kind, base + j * SW, SW, j * SW // P) for j in range(DA // SW)]
    slabs += [("v", 2 * DA + j * SW, SW, j) for j in range(DA // SW)]
    slabs += [("f", f0, P, 0)]
    for j in range(DC // SW):
        for off, kind in ((DC, "gc"), (2 * DC, "u"), (0, "gb")):
            slabs += [(kind, g0 + off + j * SW, SW, j * SW // P)]
    units = []
    for j, (kind, col, w, t0) in enumerate(slabs):
        if kind == "v":
            units += [(j, kind, 0, i, t0) for i in range(NT)]
        else:
            units += [(j, kind, ct, h, t0 + ct) for ct in range(w // P) for h in range(T // HALF)]
    last_unit = {j: n for n, (j, *_) in enumerate(units)}
    ON_ACT = ("q", "k", "v", "gc")

    def evacuated(n):
        mine = units[n][1] in ON_ACT
        return mine, sum((u[1] in ON_ACT) == mine for u in units[:n + 1])

    with ExitStack() as ctx:
        def sb(name, shape, dt, stack=ctx):
            return stack.enter_context(nc.sbuf_tensor(name, shape, dt))

        sem = s.semaphores(nc)
        raw = [s.slab[:, :, i * SW:(i + 1) * SW] for i in range(2)]
        whi = [sb(f"a_whi{i}", [P, KT, SW], F32R) for i in range(2)]
        wlo = [sb(f"a_wlo{i}", [P, KT, SW], F32R) for i in range(2)]
        hhi = sb("a_hhi", [P, KT, T], F32R)
        hlo = sb("a_hlo", [P, KT, T], F32R)
        h32 = [sb(f"a_h32_{i}", [P, HALF], F32) for i in range(2)]
        qraw = [sb(f"a_qraw{i}", [P, HALF], F32) for i in range(2)]
        sq = [sb(f"a_sq{i}", [P, HALF], F32) for i in range(2)]
        rstd = [sb(f"a_rstd{i}", [P, HALF], F32) for i in range(2)]
        stage = [sb(f"a_stage{i}", [P, HALF], F32) for i in range(2)]
        vst = [sb(f"a_vst{i}", [P, SW], F32) for i in range(2)]
        cT, ce = sb("a_cT", [P, KT], F32), sb("a_ce", [P, 2 * KT], F32)
        n1w = sb("a_n1w", [P, KT], F32)
        brow = sb("a_brow", [1, 2 * D], F32)
        mod_row = [sb(f"a_modrow{i}", [1, SW], F32) for i in range(2)]
        shift1, gain1 = sb("a_shift1", [P, KT], F32), sb("a_gain1", [P, KT], F32)
        qkw = sb("a_qkw", [P, 2], F32)
        bf = sb("a_bf", [H, 1], F32)
        cvw = sb("a_cvw", [P, 3, CT], F32)
        cnw = sb("a_cnw", [P, CT], F32)
        ss, rs = sb("a_ss", [P, NT], F32), sb("a_rs", [P, 2 * NT], F32)
        headmean = sb("a_headmean", [P, P], F32)
        chanmean = sb("a_chanmean", [P, P], F32)
        nolist = sb("a_nolist", [P, s.E * T // P, 2], I32)
        with ExitStack() as early:
            xin = sb("a_xin", [P, NT, D], F32, early)
        ucv = [sb(f"a_ucv{i}", [P, T + 2], F32) for i in range(2)]
        fz, fa, fe = (sb(f"a_f{i}", [H, HALF], F32) for i in "zae")
        cum = sb("a_cum", [H, T], F32)
        chi, clo = sb("a_chi", [H, T], F32R), sb("a_clo", [H, T], F32R)
        pone, mone = sb("a_pone", [H, T], F32), sb("a_mone", [H, T], F32)

        c_in, x_in, small_in = sem("a_c_in"), [sem(f"a_x_in{i}") for i in range(2)], sem("a_small_in")
        ada_in = [sem(f"a_ada_in{i}") for i in range(2)]
        slab_in = [sem(f"a_slab_in{i}") for i in range(2)]
        consts = sem("a_consts")
        csilu_e, csilu_ok = sem("a_csilu_e"), sem("a_csilu_ok")
        ada_mm, modrow_ok, cols_mm, mod_ok = sem("a_ada_mm"), sem("a_modrow_ok"), sem("a_cols_mm"), sem("a_mod_ok")
        squares, xnorm = sem("a_squares"), sem("a_xnorm")
        hT_mm, h32_ok, hhi_ok, hlo_ok = sem("a_hT_mm"), sem("a_h32_ok"), sem("a_hhi_ok"), sem("a_hlo_ok")
        whi_ok, wlo_ok = sem("a_whi_ok"), sem("a_wlo_ok")
        unit_mm, ev_act, ev_dve = sem("a_unit_mm"), sem("a_ev_act"), sem("a_ev_dve")
        sq_ok, ms_mm, rstd_ok, qn_ok = sem("a_sq_ok"), sem("a_ms_mm"), sem("a_rstd_ok"), sem("a_qn_ok")
        q_st = [sem(f"a_q_st{i}") for i in range(2)]
        v_st = [sem(f"a_v_st{i}") for i in range(2)]
        fz_ok, fe_ok, fl_ok, ext_ok, ext_st = sem("a_fz_ok"), sem("a_fe_ok"), sem("a_fl_ok"), sem("a_ext_ok"), sem("a_ext_st")
        ylast, csq_ok, cms_mm = sem("a_ylast"), sem("a_csq_ok"), sem("a_cms_mm")
        xrs_ok = sem("a_xrs_ok")
        dve_own, pool_own = sem("a_dve_own"), sem("a_pool_own")
        nolist_st = sem("a_nolist_st")
        qk_units = [n for n, u in enumerate(units) if u[1] in "qk"]
        v_units = [n for n, u in enumerate(units) if u[1] == "v"]
        NQK, NV = len(qk_units), len(v_units)

        def store_q(eng, k):
            j, kind, _, h, tile = units[qk_units[k]]
            dst = s.qT_d if kind == "q" else s.kT_d
            eng.wait_ge(qn_ok, k + 1)
            eng.dma_start(dst[tile * P:(tile + 1) * P, h * HALF:(h + 1) * HALF], stage[k % 2][:, :]
                          ).then_inc(q_st[k % 2], 16)

        def conv_square(eng, y):
            eng.wait_ge(csq_ok, y + 1)
            nc.tensor.matmul(psum[:, 6 + y % 2, :], chanmean[:, :], sq[y % 2][:, :], start=(y < 2),
                             stop=(y >= 2 * CT - 2), skip_group_check=True).then_inc(cms_mm, 1)

        def mod_columns(eng, r):
            eng.wait_ge(modrow_ok, r + 1)
            for q in range(SW // P):
                mm = nc.tensor.matmul(psum[:, 4, r * (SW // P) + q:r * (SW // P) + q + 1],
                                      mod_row[r % 2][:, q * P:(q + 1) * P], s.ones_row[:, 0:1],
                                      start=True, stop=True)
            mm.then_inc(cols_mm, 1)

        with nc.Block() as block:
            @block.sync
            def _(sp):
                sp.dma_start(cT[:, :], a["c"].rearrange("a (k p) -> p (a k)", p=P)).then_inc(c_in, 16)
                for r in range(NADA):
                    if r >= 2:
                        sp.wait_ge(ada_mm, r - 1)
                    sp.dma_start(raw[r % 2][:, :, :],
                                 a["w_ada"][0].rearrange("(k p) n -> p k n", p=P)[:, :, r * SW:(r + 1) * SW]
                                 ).then_inc(ada_in[r % 2], 16)
                for j, (_, col, w, _) in enumerate(slabs):
                    if j < 2:
                        sp.wait_ge(ada_mm, NADA - 1 + j)
                    else:
                        sp.wait_ge(wlo_ok, NP * (j - 1))
                    sp.dma_start(raw[j % 2][:, :, 0:w],
                                 a["w_in"][0].rearrange("(k p) n -> p k n", p=P)[:, :, col:col + w]
                                 ).then_inc(slab_in[j % 2], 16)

            @block.gpsimd
            def _(pool):
                own = Chain(pool, pool_own)
                own.link(nc.gpsimd.memset(s.ident[:, :], 0.0))
                own.link(nc.gpsimd.affine_select(out=s.ident[:, :], in_=s.ident[:, :], compare_op=ALU.not_equal,
                                                 fill=1.0, base=0, pattern=[[-1, P]], channel_multiplier=1))
                own.link(nc.gpsimd.memset(headmean[:, :], 0.0))
                for h in range(2):
                    own.link(nc.gpsimd.memset(headmean[64 * h:64 * h + 64, 64 * h:64 * h + 64], 1.0 / s.HD))
                own.link(nc.gpsimd.memset(chanmean[:, :], 1.0 / DC))
                own.link(nc.gpsimd.memset(nolist[:, :, 0:1], 0))
                own.link(nc.gpsimd.iota(nolist[:, :, 1:2].rearrange("p (a n) c -> p a (n c)", n=P),
                                        pattern=[[0, s.E * T // P // P], [1, P]], base=s.TOPK * T, channel_multiplier=0))
                own.link(nc.gpsimd.memset(s.ones_row[:, :], 1.0))
                own.link(nc.gpsimd.memset(s.eps[:, :], EPS))
                pool.sem_inc(consts, 1)
                pool.dma_start(s.list_d.rearrange("(p n) a -> p n a", p=P), nolist[:, :, :]).then_inc(nolist_st, 16)
                for k, n in enumerate(qk_units):
                    if k >= 2:
                        pool.wait_ge(ms_mm, k - 1)
                    pool.wait_ge(ev_act, evacuated(n)[1])
                    nc.gpsimd.tensor_tensor(sq[k % 2][:, :], qraw[k % 2][:, :], qraw[k % 2][:, :],
                                            ALU.mult).then_inc(sq_ok, 1)
                    if k >= 2:
                        store_q(pool, k - 2)
                store_q(pool, NQK - 2)
                store_q(pool, NQK - 1)
                for m, n in enumerate(v_units):
                    j, _, _, i, t0 = units[n]
                    pool.wait_ge(ev_act, evacuated(n)[1])
                    pool.dma_start(s.v_d[i * P:(i + 1) * P, t0 * SW:(t0 + 1) * SW], vst[m % 2][:, :]
                                   ).then_inc(v_st[m % 2], 16)
                pool.wait_ge(hT_mm, 16)
                own.link(nc.gpsimd.memset(pone[:, :], 1.0))
                own.link(nc.gpsimd.memset(mone[:, :], -1.0))
                for i in range(2):
                    own.link(nc.gpsimd.memset(ucv[i][:, 0:2], 0.0))
                pool.sem_inc(consts, 1)
                pool.wait_ge(ext_ok, 2)
                for r, (qs, ks) in enumerate(((chi, pone), (clo, pone), (mone, chi), (mone, clo))):
                    for dst, src in ((s.extq_d, qs), (s.extk_d, ks)):
                        v = src[:, :].bitcast(F32) if src in (chi, clo) else src[:, :]
                        pool.dma_start(dst[:, r, :], v).then_inc(ext_st, 16)
                for k in range(2 * CT):
                    ct, h = k // 2, k % 2
                    pool.wait_ge(ylast, k + 1)
                    if k >= 2:
                        pool.wait_ge(cms_mm, k - 1)
                    nc.gpsimd.tensor_tensor(sq[k % 2][:, :], s.convn[:, ct, h * HALF:(h + 1) * HALF],
                                            s.convn[:, ct, h * HALF:(h + 1) * HALF], ALU.mult).then_inc(csq_ok, 1)
                pool.wait_ge(ext_st, 16 * 8)
                pool.wait_ge(nolist_st, 16)
                for i in range(2):
                    pool.wait_ge(q_st[i], 16 * NQK // 2)
                    pool.wait_ge(v_st[i], 16 * NV // 2)

            @block.scalar
            def _(act):
                for i in range(2):
                    act.dma_start(xin[:, 4 * i:4 * i + 4, :],
                                  a["x"][0, 512 * i:512 * i + 512, :].rearrange("(t p) d -> p t d", p=P)
                                  ).then_inc(x_in[i], 16)
                col = lambda v, n: v.rearrange("a (k p) -> p (a k)", p=n)
                loads = [(n1w[:, :], col(a["norm1_w"], P)), (bf[:, :], col(a["b_forget"], H)),
                         (cnw[:, :], col(a["conv_out_norm_w"], P)), (brow[:, :], a["b_ada"][0:1, 0:2 * D])]
                loads += [(cvw[:, j, :], col(a["conv_w"][0, j:j + 1, :], P)) for j in range(3)]
                for h in range(2):
                    loads += [(qkw[64 * h:64 * h + 64, 0:1], col(a["q_norm_w"], 64)),
                              (qkw[64 * h:64 * h + 64, 1:2], col(a["k_norm_w"], 64))]
                for dst, src in loads:
                    act.dma_start(dst, src).then_inc(small_in, 16)
                act.wait_ge(c_in, 16)
                nc.scalar.activation(ce[:, 0:KT], cT[:, :], ACT.Exp, scale=-1.0).then_inc(csilu_e, 1)
                for i in range(NT):
                    act.wait_ge(x_in[i // 4], 16)
                    if i >= 1:
                        act.wait_ge(squares, i)
                    nc.scalar.activation(s.convn[:, 0, :], xin[:, i, :], ACT.Square,
                                         accum_out=ss[:, i:i + 1]).then_inc(squares, 1)
                    if i % 4 == 3:
                        act.wait_ge(squares, i + 1)
                        act.wait_ge(consts, 1)
                        nc.scalar.activation(rs[:, i - 3:i + 1], ss[:, i - 3:i + 1], ACT.Sqrt, bias=s.eps[:, :],
                                             scale=1.0 / D).then_inc(xrs_ok, 1)

                def split_hi(j):
                    w = slabs[j][2]
                    act.wait_ge(slab_in[j % 2], 16 * (j // 2 + 1))
                    if j >= 2:
                        act.wait_ge(unit_mm, last_unit[j - 2] + 1)
                    for q in range(NP):
                        nc.scalar.activation(whi[j % 2][:, PIECE * q:PIECE * (q + 1), 0:w],
                                             raw[j % 2][:, PIECE * q:PIECE * (q + 1), 0:w],
                                             ACT.Copy).then_inc(whi_ok, 1)

                for u in range(2):
                    for kt in range(KT):
                        n = KT * u + kt
                        act.wait_ge(h32_ok, n + 1)
                        nc.scalar.activation(hhi[:, kt, u * HALF:(u + 1) * HALF], h32[n % 2][:, :],
                                             ACT.Copy).then_inc(hhi_ok, 1)
                    split_hi(u)

                def root(k, bank):
                    if k >= 2:
                        act.wait_ge(qn_ok, k - 1)
                    nc.scalar.activation(rstd[k % 2][:, :], psum[:, bank + k % 2, :], ACT.Sqrt,
                                         bias=s.eps[:, :]).then_inc(rstd_ok, 1)

                k = m = 0
                for n, (j, kind, ct, h, tile) in enumerate(units):
                    if n and units[n - 1][0] != j and 1 <= j < len(slabs) - 1:
                        split_hi(j + 1)
                    act.wait_ge(unit_mm, n + 1) if kind in ON_ACT or kind == "f" else None
                    src = psum[:, n % 4, :]
                    if kind in "qk":
                        if k >= 2:
                            act.wait_ge(qn_ok, k - 1)
                        nc.scalar.activation(qraw[k % 2][:, :], src, ACT.Copy).then_inc(ev_act, 1)
                        k += 1
                    elif kind == "v":
                        if m >= 2:
                            act.wait_ge(v_st[m % 2], 16 * (m // 2))
                        nc.scalar.activation(vst[m % 2][:, :], src[:, 0:SW], ACT.Copy).then_inc(ev_act, 1)
                        m += 1
                    elif kind == "gc":
                        act.wait_ge(squares, NT)
                        nc.scalar.activation(s.convn[:, tile, h * HALF:(h + 1) * HALF], src,
                                             ACT.Copy).then_inc(ev_act, 1)
                    elif kind == "f":
                        act.wait_ge(fz_ok, 3 * h + 3)
                        nc.scalar.activation(fe[:, :], fa[:, :], ACT.Exp, scale=-1.0).then_inc(fe_ok, 1)
                        act.wait_ge(fe_ok, 2 * h + 1)
                        nc.scalar.activation(fa[:, :], fe[:, :], ACT.Ln, bias=1.0).then_inc(fe_ok, 1)
                    if n and units[n - 1][1] in "qk":
                        act.wait_ge(ms_mm, n)
                        root(n - 1, 4)
                for h in range(2):
                    act.wait_ge(cms_mm, 2 * CT - 1 + h)
                    root(NQK + h, 6)

            @block.vector
            def _(dve):
                own = Chain(dve, dve_own)
                dve.wait_ge(csilu_e, 1)
                own.link(nc.vector.tensor_scalar(ce[:, KT:2 * KT], ce[:, 0:KT], 1.0, None, ALU.add))
                own.link(nc.vector.reciprocal(ce[:, 0:KT], ce[:, KT:2 * KT]))
                nc.vector.tensor_tensor(s.csilu[:, :], cT[:, :], ce[:, 0:KT], ALU.mult).then_inc(csilu_ok, 1)

                def xn(i):
                    if i % 4 == 0:
                        dve.wait_ge(xrs_ok, i // 4 + 1)
                        own.link(nc.vector.reciprocal(rs[:, NT + i:NT + i + 4], rs[:, i:i + 4]))
                    nc.vector.tensor_scalar(xin[:, i, :], xin[:, i, :], rs[:, NT + i:NT + i + 1], None,
                                            ALU.mult).then_inc(xnorm, 1)

                for i in range(NT):
                    xn(i)
                dve.wait_ge(small_in, 16 * 11)
                for r in range(NADA):
                    dve.wait_ge(ada_mm, r + 1)
                    if r >= 2:
                        dve.wait_ge(cols_mm, r - 1)
                    nc.vector.tensor_tensor(mod_row[r % 2][:, :], psum[0:1, r % 4, 0:SW],
                                            brow[:, r * SW:(r + 1) * SW], ALU.add).then_inc(modrow_ok, 1)
                dve.wait_ge(cols_mm, NADA)
                nc.vector.tensor_copy(shift1[:, :], psum[:, 4, 0:KT]).then_inc(mod_ok, 1)
                nc.vector.scalar_tensor_tensor(gain1[:, :], psum[:, 4, KT:2 * KT], 1.0, n1w[:, :],
                                               ALU.add, ALU.mult).then_inc(mod_ok, 1)
                dve.wait_ge(mod_ok, 2)

                def split_lo(j):
                    w = slabs[j][2]
                    for q in range(NP):
                        dve.wait_ge(whi_ok, NP * j + q + 1)
                        part = slice(PIECE * q, PIECE * (q + 1))
                        nc.vector.tensor_tensor(wlo[j % 2][:, part, 0:w], raw[j % 2][:, part, 0:w],
                                                whi[j % 2][:, part, 0:w].bitcast(F32), ALU.subtract).then_inc(wlo_ok, 1)

                def h_lo(n):
                    u, kt = n // KT, n % KT
                    dve.wait_ge(hhi_ok, n + 1)
                    nc.vector.tensor_tensor(hlo[:, kt, u * HALF:(u + 1) * HALF], h32[n % 2][:, :],
                                            hhi[:, kt, u * HALF:(u + 1) * HALF].bitcast(F32),
                                            ALU.subtract).then_inc(hlo_ok, 1)

                for u in range(2):
                    for kt in range(KT):
                        n = KT * u + kt
                        dve.wait_ge(hT_mm, n + 1)
                        if n >= 2:
                            dve.wait_ge(hlo_ok, n - 1)
                        nc.vector.tensor_scalar(h32[n % 2][:, :], psum[:, 5 + n % 3, :], gain1[:, kt:kt + 1],
                                                shift1[:, kt:kt + 1], ALU.mult, ALU.add).then_inc(h32_ok, 1)
                        if kt:
                            h_lo(n - 1)
                    h_lo(KT * u + KT - 1)
                    split_lo(u)

                def norm_qk(k):
                    kind = units[qk_units[k]][1]
                    dve.wait_ge(rstd_ok, k + 1)
                    own.link(nc.vector.reciprocal(rstd[k % 2][:, :], rstd[k % 2][:, :]))
                    if k >= 2:
                        dve.wait_ge(q_st[k % 2], 16 * (k // 2))
                    w = 0 if kind == "q" else 1
                    nc.vector.scalar_tensor_tensor(stage[k % 2][:, :], qraw[k % 2][:, :], qkw[:, w:w + 1],
                                                   rstd[k % 2][:, :], ALU.mult, ALU.mult).then_inc(qn_ok, 1)

                k = y = 0
                for n, (j, kind, ct, h, tile) in enumerate(units):
                    if n and units[n - 1][0] != j and 1 <= j < len(slabs) - 1:
                        split_lo(j + 1)
                    if kind in "qk" or (kind == "v" and k < NQK):
                        if n >= 1 and k < NQK:
                            norm_qk(k)
                            k += 1
                    src = psum[:, n % 4, :]
                    part = slice(h * HALF, (h + 1) * HALF)
                    if kind == "f":
                        dve.wait_ge(unit_mm, n + 1)
                        if h:
                            dve.wait_ge(fl_ok, 1)
                        nc.vector.tensor_scalar(fz[:, :], src[0:H, :], bf[:, 0:1], None, ALU.add).then_inc(fz_ok, 1)
                        dve.wait_ge(fz_ok, 3 * h + 1)
                        nc.vector.scalar_tensor_tensor(fa[:, :], fz[:, :], -1.0, fz[:, :], ALU.mult,
                                                       ALU.max).then_inc(fz_ok, 1)
                        dve.wait_ge(fz_ok, 3 * h + 2)
                        nc.vector.tensor_scalar(fz[:, :], fz[:, :], 0.0, None, ALU.min).then_inc(fz_ok, 1)
                        dve.wait_ge(fe_ok, 2 * h + 2)
                        own.link(nc.vector.tensor_tensor(fz[:, :], fz[:, :], fa[:, :], ALU.subtract))
                        dve.wait_ge(consts, 2)
                        first = 0.0 if h == 0 else cum[:, HALF - 1:HALF]
                        own.link(nc.vector.tensor_tensor_scan(cum[:, part], pone[:, part], fz[:, :], first,
                                                              ALU.mult, ALU.add))
                        dve.sem_inc(fl_ok, 1)
                        dve.sem_inc(ev_dve, 1)
                        if h:
                            own.link(nc.vector.tensor_scalar(cum[:, :], cum[:, :], float(s.HD) ** 0.5, None, ALU.mult))
                            own.link(nc.vector.tensor_copy(chi[:, :], cum[:, :]))
                            nc.vector.tensor_tensor(clo[:, :], cum[:, :], chi[:, :].bitcast(F32),
                                                    ALU.subtract).then_inc(ext_ok, 2)
                    elif kind == "u":
                        dve.wait_ge(unit_mm, n + 1)
                        own.link(nc.vector.tensor_tensor(ucv[tile % 2][:, 2 + h * HALF:2 + (h + 1) * HALF], src,
                                                         s.convn[:, tile, part], ALU.mult))
                        dve.sem_inc(ev_dve, 1)
                        if h:
                            uc = ucv[tile % 2]
                            own.link(nc.vector.tensor_scalar(s.convn[:, tile, :], uc[:, 0:T], cvw[:, 0, tile:tile + 1],
                                                             None, ALU.mult))
                            for tap in (1, 2):
                                own.link(nc.vector.scalar_tensor_tensor(s.convn[:, tile, :], uc[:, tap:tap + T],
                                                                        cvw[:, tap, tile:tile + 1], s.convn[:, tile, :],
                                                                        ALU.mult, ALU.add))
                    elif kind == "gb":
                        dve.wait_ge(unit_mm, n + 1)
                        own.link(nc.vector.tensor_tensor(s.convn[:, tile, part], src, s.convn[:, tile, part], ALU.mult))
                        dve.sem_inc(ev_dve, 1)
                        dve.sem_inc(ylast, 1)
                dve.wait_ge(csq_ok, 2 * CT)
                for h in range(2):
                    dve.wait_ge(rstd_ok, NQK + 1 + h)
                    own.link(nc.vector.reciprocal(rstd[h][:, :], rstd[h][:, :]))
                    for ct in range(CT):
                        part = slice(h * HALF, (h + 1) * HALF)
                        own.link(nc.vector.scalar_tensor_tensor(s.convn[:, ct, part], s.convn[:, ct, part],
                                                                cnw[:, ct:ct + 1], rstd[h][:, :], ALU.mult, ALU.mult))

            @block.tensor
            def _(pe):
                pe.wait_ge(csilu_ok, 1)
                pe.wait_ge(consts, 1)
                for r in range(NADA):
                    pe.wait_ge(ada_in[r % 2], 16 * (r // 2 + 1))
                    if r >= 4:
                        pe.wait_ge(modrow_ok, r - 3)
                    for k in range(KT):
                        mm = nc.tensor.matmul(psum[0:1, r % 4, 0:SW], s.csilu[:, k:k + 1], raw[r % 2][:, k, :],
                                              start=(k == 0), stop=(k == KT - 1))
                    mm.then_inc(ada_mm, 1)
                    if r:
                        mod_columns(pe, r - 1)
                mod_columns(pe, NADA - 1)
                for u in range(2):
                    pe.wait_ge(xnorm, 4 * (u + 1))
                    for kt in range(KT):
                        n = KT * u + kt
                        if n >= 3:
                            pe.wait_ge(h32_ok, n - 2)
                        for t in range(4):
                            mm = nc.tensor.transpose(psum[:, 5 + n % 3, t * P:(t + 1) * P],
                                                     xin[:, 4 * u + t, kt * P:(kt + 1) * P], s.ident[:, :])
                        mm.then_inc(hT_mm, 1)
                pe.wait_ge(hlo_ok, 2 * KT)
                k = 0
                for n, (j, kind, ct, h, tile) in enumerate(units):
                    if n == 0 or units[n - 1][0] != j:
                        pe.wait_ge(wlo_ok, NP * (j + 1))
                    if n >= 4:
                        mine, count = evacuated(n - 4)
                        pe.wait_ge(ev_act if mine else ev_dve, count)
                    steps = [(x_, w_, kt) for kt in range(KT) for x_, w_ in ((hhi, whi), (hhi, wlo), (hlo, whi))]
                    for q, (hx, wx, kt) in enumerate(steps):
                        st, sp_ = q == 0, q == len(steps) - 1
                        if kind == "v":
                            mm = nc.tensor.matmul(psum[:, n % 4, 0:SW], hx[:, kt, h * P:(h + 1) * P],
                                                  wx[j % 2][:, kt, :], start=st, stop=sp_)
                        else:
                            mm = nc.tensor.matmul(psum[:, n % 4, :], wx[j % 2][:, kt, ct * P:(ct + 1) * P],
                                                  hx[:, kt, h * HALF:(h + 1) * HALF], start=st, stop=sp_)
                    mm.then_inc(unit_mm, 1)
                    if n and units[n - 1][1] in "qk":
                        pe.wait_ge(sq_ok, k + 1)
                        if k >= 2:
                            pe.wait_ge(rstd_ok, k - 1)
                        nc.tensor.matmul(psum[:, 4 + k % 2, :], headmean[:, :], sq[k % 2][:, :],
                                         start=True, stop=True).then_inc(ms_mm, 1)
                        k += 1
                    if kind == "gb":
                        y = 2 * tile + h - 1
                        if y >= 0:
                            conv_square(pe, y)
                conv_square(pe, 2 * CT - 1)

def attention_block(nc, s, a):
    T, D, NT, KT, H, HD = s.T, s.D, s.NT, s.KT, s.H, s.HD
    psum = s.psum
    SL = 512
    STEPS = 2 * NT
    chunks = []
    for n in range(STEPS):
        for k0 in range(0, n % NT + 1, 4):
            chunks.append((n, k0, min(4, n % NT + 1 - k0)))
    NCH = len(chunks)
    of = lambda n: [m for m in range(NCH) if chunks[m][0] == n]
    through = lambda n: of(n)[-1] + 1
    R = 4
    assert NCH % R == 0 and NT == KT
    with ExitStack() as ctx:
        def sb(name, shape, dt):
            return ctx.enter_context(nc.sbuf_tensor(name, shape, dt))

        sem = s.semaphores(nc)
        raw = [sb(f"b_raw{i}", [P, KT, SL], F32) for i in range(2)]
        brow = sb("b_brow", [1, 4 * D], F32)
        qf = [sb(f"b_qf{i}", [P, T], F32) for i in range(2)]
        kf = [sb(f"b_kf{i}", [P, T], F32) for i in range(2)]
        q1 = [sb(f"b_q1_{i}", [P, T], F32R) for i in range(2)]
        k1 = [sb(f"b_k1_{i}", [P, T], F32R) for i in range(2)]
        q2 = [sb(f"b_q2_{i}", [P, T], F32R) for i in range(2)]
        k2 = [sb(f"b_k2_{i}", [P, T], F32R) for i in range(2)]
        vraw = sb("b_vraw", [P, NT, 2 * HD], F32)
        vhl = sb("b_vhl", [P, NT, 2, 2 * HD], F32R)
        pr = [sb(f"b_pr{i}", [P, T], F32) for i in range(2)]
        pthi = [sb(f"b_pthi{i}", [P, 4 * P], F32R) for i in range(R)]
        ptlo = [sb(f"b_ptlo{i}", [P, 4 * P], F32R) for i in range(R)]
        mx, nb = sb("b_mx", [P, STEPS], F32), sb("b_nb", [P, STEPS], F32)
        rsum, rl = sb("b_rsum", [P, STEPS], F32), sb("b_rl", [P, STEPS], F32)
        otmp = [sb(f"b_otmp{i}", [P, HD], F32) for i in range(2)]
        mask32 = sb("b_mask32", [P, P], F32)

        qk_in = [sem(f"b_qk_in{i}") for i in range(2)]
        ext_in = [sem(f"b_ext_in{i}") for i in range(2)]
        v_in, brow_in, slab_in = sem("b_v_in"), sem("b_brow_in"), sem("b_slab_in")
        ada_in = [sem(f"b_ada_in{i}") for i in range(2)]
        mask_ok, mask_r = sem("b_mask_ok"), sem("b_mask_r")
        prep_hi = [sem(f"b_prep_hi{i}") for i in range(2)]
        prep_lo = [sem(f"b_prep_lo{i}") for i in range(2)]
        v_hi, v_lo = sem("b_v_hi"), sem("b_v_lo")
        ada_mm, mod_ok = sem("b_ada_mm"), sem("b_mod_ok")
        s_mm, nb_ok, mx_ok, exp_ok = sem("b_s_mm"), sem("b_nb_ok"), sem("b_mx_ok"), sem("b_exp_ok")
        pt_mm, pthi_ok, ptlo_ok, pv_mm = sem("b_pt_mm"), sem("b_pthi_ok"), sem("b_ptlo_ok"), sem("b_pv_mm")
        ot_ok, o_ok = sem("b_ot_ok"), sem("b_o_ok")

        with nc.Block() as block:
            @block.sync
            def _(sp):
                sp.dma_start(brow[:, :], a["b_ada"][0:1, 2 * D:6 * D]).then_inc(brow_in, 16)
                sp.wait_ge(mask_r, 4)

                def load(p, later):
                    for i in range(2):
                        if i == 0:
                            if later:
                                sp.wait_ge(v_lo, p)
                            sp.dma_start(vraw[:, :, :], s.v_d.rearrange("(t p) (g n) -> p t g n", p=P, n=2 * HD)
                                         [:, :, bass.ds(p, 1), :].rearrange("p t g n -> p t (g n)")).then_inc(v_in, 16)
                        if later:
                            sp.wait_ge(prep_lo[i], 2 * p)
                        row = (2 * p + i) * HD
                        for half in (0, HD):
                            sp.dma_start(qf[i][half:half + HD, :], s.qT_d[bass.ds(row, HD), :]).then_inc(qk_in[i], 16)
                            sp.dma_start(kf[i][half:half + HD, :], s.kT_d[bass.ds(row, HD), :]).then_inc(qk_in[i], 16)
                        if later:
                            sp.wait_ge(s_mm, STEPS * p - NT * (1 - i))
                        for dst, src in ((q2, s.extq_d), (k2, s.extk_d)):
                            sp.dma_start(dst[i][HD:HD + 4, :].bitcast(F32),
                                         src[bass.ds(2 * p + i, 1), :, :].rearrange("a r t -> (a r) t")
                                         ).then_inc(ext_in[i], 16)
                        if later:
                            sp.wait_ge(ada_mm, 2 * p - 1 + i)
                        sp.dma_start(raw[i][:, :, :], a["w_ada"][0].rearrange("(k p) n -> p k n", p=P)
                                     [:, :, bass.ds(2 * D + (2 * p + i) * SL, SL)]).then_inc(ada_in[i], 16)

                load(0, False)
                with sp.Fori(1, H // 2) as p:
                    load(p, True)
                sp.dma_start(s.slab[:, :, :], a["w_out"][0].rearrange("(k p) n -> p k n", p=P)[:, :, 0:s.HALF]
                             ).then_inc(slab_in, 16)
                sp.wait_ge(slab_in, 16)

            @block.gpsimd
            def _(pool):
                nc.gpsimd.memset(mask32[:, :], 0.0).then_inc(mask_ok, 1)
                pool.wait_ge(mask_ok, 1)
                nc.gpsimd.affine_select(out=mask32[:, :], in_=mask32[:, :], compare_op=ALU.is_ge, fill=NEG, base=0,
                                        pattern=[[-1, P]], channel_multiplier=1).then_inc(mask_ok, 1)

            @block.scalar
            def _(act):
                def prep(i, p):
                    act.wait_ge(qk_in[i], 64 * (p + 1))
                    nc.scalar.activation(q1[i][:, :], qf[i][:, :], ACT.Copy).then_inc(prep_hi[i], 1)
                    nc.scalar.activation(k1[i][:, :], kf[i][:, :], ACT.Copy).then_inc(prep_hi[i], 1)
                    nc.scalar.activation(q2[i][0:HD, :], qf[i][0:HD, :], ACT.Copy).then_inc(prep_hi[i], 1)

                prep(0, 0)
                with act.Fori(0, H // 2) as p:
                    def exp(n):
                        i, L = n % NT, (n % NT + 1) * P
                        act.wait_ge(nb_ok, STEPS * p + n + 1)
                        if n >= 2:
                            act.wait_ge(pt_mm, NCH * p + through(n - 2))
                        sc = psum[:, 2 * (n % 2):2 * (n % 2) + 2, :].rearrange("p b n -> p (b n)")[:, 0:L]
                        nc.scalar.activation(pr[n % 2][:, 0:L], sc, ACT.Exp, bias=nb[:, n:n + 1], scale=HD ** -0.5,
                                             accum_out=rsum[:, n:n + 1]).then_inc(exp_ok, 1)

                    exp(0)
                    act.wait_ge(v_in, 16 * (p + 1))
                    vv = vraw[:, :, :].rearrange("p t (g n) -> p (t g) n", n=HD)
                    nc.scalar.activation(vhl[:, :, :, :].rearrange("p t g n -> p (t g) n")[:, :, 0:HD], vv,
                                         ACT.Copy).then_inc(v_hi, 1)
                    for n in range(STEPS):
                        if n == 1:
                            prep(1, p)
                        if n == NT + 2:
                            act.wait_ge(s_mm, STEPS * p + NT)
                            s.settle(act)
                            with act.If(p < H // 2 - 1):
                                prep(0, p + 1)
                        for m in of(n):
                            w = chunks[m][2] * P
                            act.wait_ge(pt_mm, NCH * p + m + 1)
                            if m >= R:
                                act.wait_ge(pv_mm, NCH * p + m - R + 1)
                            nc.scalar.activation(pthi[m % R][:, 0:w], psum[:, 4 + m % 2, 0:w],
                                                 ACT.Copy).then_inc(pthi_ok, 1)
                        if n + 1 < STEPS:
                            exp(n + 1)
                    act.wait_ge(pv_mm, NCH * (p + 1))
                    s.settle(act)

            @block.vector
            def _(dve):
                for i in range(2):
                    nc.vector.memset(q2[i][HD:P, :].bitcast(F32), 0.0).then_inc(mask_r, 1)
                    nc.vector.memset(k2[i][HD:P, :].bitcast(F32), 0.0).then_inc(mask_r, 1)
                dve.wait_ge(mask_ok, 2)
                nc.vector.tensor_copy(s.mask[:, :], mask32[:, :]).then_inc(mask_r, 1)
                nc.vector.tensor_copy(s.ident_r[:, :], s.ident[:, :]).then_inc(mask_r, 1)
                dve.wait_ge(brow_in, 16)
                def prep(i, p):
                    dve.wait_ge(prep_hi[i], 3 * p + 1)
                    lower = slice(HD, P)
                    nc.vector.tensor_tensor(q1[i][lower, :], qf[i][lower, :], q1[i][lower, :].bitcast(F32),
                                            ALU.subtract).then_inc(prep_lo[i], 1)
                    dve.wait_ge(prep_hi[i], 3 * p + 3)
                    nc.vector.tensor_tensor(k2[i][0:HD, :], kf[i][0:HD, :], k1[i][0:HD, :].bitcast(F32),
                                            ALU.subtract).then_inc(prep_lo[i], 1)

                prep(0, 0)
                with dve.Fori(0, H // 2) as p:
                    def top(n):
                        L = (n % NT + 1) * P
                        sc = psum[:, 2 * (n % 2):2 * (n % 2) + 2, :].rearrange("p b n -> p (b n)")[:, 0:L]
                        dve.wait_ge(s_mm, STEPS * p + n + 1)
                        nc.vector.reduce_max(mx[:, n:n + 1], sc, AX_X).then_inc(mx_ok, 1)
                        dve.wait_ge(mx_ok, STEPS * p + n + 1)
                        nc.vector.tensor_scalar(nb[:, n:n + 1], mx[:, n:n + 1], -HD ** -0.5, None,
                                                ALU.mult).then_inc(nb_ok, 1)

                    def modulation(i):
                        dve.wait_ge(ada_mm, 2 * p + i + 1)
                        at = bass.ds((2 * p + i) * SL, SL)
                        nc.vector.tensor_tensor(s.modrow[:, at], psum[0:1, 7, :], brow[:, at],
                                                ALU.add).then_inc(mod_ok, 1)

                    def finish(n):
                        i, g = n % NT, n // NT
                        dve.wait_ge(pv_mm, NCH * p + through(n))
                        nc.vector.reciprocal(rl[:, n:n + 1], rsum[:, n:n + 1]).then_inc(ot_ok, 1)
                        dve.wait_ge(ot_ok, 2 * (STEPS * p + n) + 1)
                        nc.vector.tensor_scalar(otmp[n % 2][:, :], psum[:, 6, HD:2 * HD], rl[:, n:n + 1],
                                                None, ALU.mult).then_inc(ot_ok, 1)
                        dve.wait_ge(ot_ok, 2 * (STEPS * p + n) + 2)
                        nc.vector.scalar_tensor_tensor(s.attn[:, i, bass.ds(2 * HD * p + g * HD, HD)],
                                                       psum[:, 6, 0:HD], rl[:, n:n + 1], otmp[n % 2][:, :],
                                                       ALU.mult, ALU.add).then_inc(o_ok, 1)

                    top(0)
                    top(1)
                    dve.wait_ge(v_hi, p + 1)
                    vv = vraw[:, :, :].rearrange("p t (g n) -> p (t g) n", n=HD)
                    vo = vhl[:, :, :, :].rearrange("p t g n -> p (t g) n")
                    nc.vector.tensor_tensor(vo[:, :, HD:2 * HD], vv, vo[:, :, 0:HD].bitcast(F32),
                                            ALU.subtract).then_inc(v_lo, 1)
                    for n in range(STEPS):
                        if n == 2:
                            prep(1, p)
                        if n == NT + 3:
                            s.settle(dve)
                            with dve.If(p < H // 2 - 1):
                                prep(0, p + 1)
                        for m in of(n):
                            w = chunks[m][2] * P
                            dve.wait_ge(pthi_ok, NCH * p + m + 1)
                            nc.vector.tensor_tensor(ptlo[m % R][:, 0:w], psum[:, 4 + m % 2, 0:w],
                                                    pthi[m % R][:, 0:w].bitcast(F32), ALU.subtract).then_inc(ptlo_ok, 1)
                        if n + 2 < STEPS:
                            top(n + 2)
                        if n:
                            finish(n - 1)
                        if n % NT == NT - 1:
                            modulation(n // NT)
                    finish(STEPS - 1)

            @block.tensor
            def _(pe):
                pe.wait_ge(mask_r, 6)
                with pe.Fori(0, H // 2) as p:
                    def modulation(n):
                        i, k = n // NT, n % NT
                        if k == 0:
                            pe.wait_ge(ada_in[i], 16 * (p + 1))
                            pe.wait_ge(mod_ok, 2 * p + 1) if i else pe.wait_ge(v_lo, p + 1)
                        mm = nc.tensor.matmul(psum[0:1, 7, :], s.csilu[:, k:k + 1], raw[i][:, k, :],
                                              start=(k == 0), stop=(k == KT - 1))
                        if k == KT - 1:
                            mm.then_inc(ada_mm, 1)

                    def scores(n):
                        i, g = n % NT, n // NT
                        if i == 0:
                            pe.wait_ge(prep_lo[g], 2 * (p + 1))
                            pe.wait_ge(ext_in[g], 32 * (p + 1))
                        if n >= 2:
                            pe.wait_ge(exp_ok, STEPS * p + n - 1)
                        L = (i + 1) * P
                        for c0 in range(0, L, 512):
                            w = min(512, L - c0)
                            to = psum[:, 2 * (n % 2) + c0 // 512, 0:w]
                            diag = c0 + w == L
                            rows = slice(i * P, (i + 1) * P)
                            nc.tensor.matmul(to, q1[g][:, rows], k1[g][:, c0:c0 + w], start=True, stop=False)
                            mm = nc.tensor.matmul(to, q2[g][:, rows], k2[g][:, c0:c0 + w], start=False, stop=not diag)
                            if diag:
                                mm = nc.tensor.matmul(to[:, w - P:w], s.ident_r[:, :], s.mask[:, :],
                                                      start=False, stop=True)
                        mm.then_inc(s_mm, 1)

                    def turn(n):
                        pe.wait_ge(exp_ok, STEPS * p + n + 1)
                        for m in of(n):
                            _, k0, cnt = chunks[m]
                            if m >= 2:
                                pe.wait_ge(ptlo_ok, NCH * p + m - 1)
                            for t in range(cnt):
                                mm = nc.tensor.transpose(psum[:, 4 + m % 2, t * P:(t + 1) * P],
                                                         pr[n % 2][:, (k0 + t) * P:(k0 + t + 1) * P], s.ident[:, :])
                            mm.then_inc(pt_mm, 1)

                    def values(n):
                        i, g = n % NT, n // NT
                        if n == 0:
                            pe.wait_ge(v_lo, p + 1)
                        else:
                            pe.wait_ge(o_ok, STEPS * p + n)
                        for m in of(n):
                            _, k0, cnt = chunks[m]
                            pe.wait_ge(ptlo_ok, NCH * p + m + 1)
                            for t in range(cnt):
                                kt = k0 + t
                                cols = slice(t * P, (t + 1) * P)
                                nc.tensor.matmul(psum[:, 6, 0:2 * HD], pthi[m % R][:, cols], vhl[:, kt, g, :],
                                                 start=(kt == 0), stop=False)
                                mm = nc.tensor.matmul(psum[:, 6, 0:HD], ptlo[m % R][:, cols],
                                                      vhl[:, kt, g, 0:HD], start=False, stop=(kt == i))
                            mm.then_inc(pv_mm, 1)

                    scores(0)
                    scores(1)
                    for n in range(STEPS):
                        turn(n)
                        if n + 2 < STEPS:
                            scores(n + 2)
                        modulation(n)
                        if n:
                            values(n - 1)
                    values(STEPS - 1)


def mixer_block(nc, s, a):
    T, D, NT, KT, CT, E, K4 = s.T, s.D, s.NT, s.KT, s.CT, s.E, s.TOPK
    psum = s.psum
    SL = 512
    NS = D // SL
    PIECE = 2
    NP = KT // PIECE
    with ExitStack() as ctx:
        def sb(name, shape, dt):
            return ctx.enter_context(nc.sbuf_tensor(name, shape, dt))

        sem = s.semaphores(nc)
        wraw = s.slab
        whi = [sb(f"c_whi{i}", [P, KT, SL], F32R) for i in range(NS)]
        wlo = [sb(f"c_wlo{i}", [P, KT, SL], F32R) for i in range(NS)]
        gate1 = sb("c_gate1", [P, D], F32)
        awbc = sb("c_awbc", [P, s.DA], F32)
        n2w = sb("c_n2w", [P, KT], F32)
        wr = sb("c_wr", [P, KT, E], F32)
        brbc = sb("c_brbc", [P, E], F32)
        xt = [sb(f"c_xt{i}", [P, D], F32) for i in range(2)]
        an = [sb(f"c_an{i}", [P, s.DA], F32) for i in range(2)]
        athi = [sb(f"c_athi{i}", [P, s.DA], F32R) for i in range(2)]
        atlo = [sb(f"c_atlo{i}", [P, s.DA], F32R) for i in range(2)]
        cthi = [sb(f"c_cthi{i}", [P, CT, P], F32R) for i in range(2)]
        ctlo = [sb(f"c_ctlo{i}", [P, CT, P], F32R) for i in range(2)]
        xn2 = [sb(f"c_xn2_{i}", [P, D], F32) for i in range(2)]
        h2T = [sb(f"c_h2T{i}", [P, KT, P], F32) for i in range(2)]
        dump, adump = sb("c_dump", [P, D], F32), sb("c_adump", [P, s.DA], F32)
        st = [sb(f"c_st{i}", [P, 8], F32) for i in range(2)]
        lg = sb("c_lg", [P, E], F32)
        top, topi = sb("c_top", [P, 8], F32), sb("c_topi", [P, 8], U32)
        topf, topsum = sb("c_topf", [P, K4], F32), sb("c_topsum", [P, 2 * NT], F32)
        hot, hotpos = sb("c_hot", [P, K4, E], F32), sb("c_hotpos", [P, K4, E], F32)
        pos, slotf = sb("c_pos", [P, E], F32), sb("c_slotf", [P, 2 * K4], F32)
        sel = [sb(f"c_sel{i}", [P, E], BF16) for i in range(2)]
        sel_before = sb("c_sel_before", [P, E], BF16)
        tri, ones_bf = sb("c_tri", [P, P], BF16), sb("c_ones_bf", [P, P], BF16)
        iota_e = sb("c_iota_e", [P, E], F32)
        entry = [[sb(f"c_entry{i}_{r}", [P, 2], I32) for r in range(K4)] for i in range(2)]
        tokf = sb("c_tokf", [P, NT], F32)
        slot = [[sb(f"c_slot{i}_{r}", [P, 1], I32) for r in range(K4)] for i in range(2)]
        cnt = sb("c_cnt", [1, 6 * E], F32)

        w_in, small_in, slab_in = sem("c_w_in"), sem("c_small_in"), sem("c_slab_in")
        x_in = [sem(f"c_x_in{i}") for i in range(2)]
        whi_ok, wlo_ok = sem("c_whi_ok"), sem("c_wlo_ok")
        consts, pool_own = sem("c_consts"), sem("c_pool_own")
        bc_mm, bc_ok, cols_mm, cols_ok = sem("c_bc_mm"), sem("c_bc_ok"), sem("c_cols_mm"), sem("c_cols_ok")
        assq, an_ok, at_mm, athi_ok, at_ok = sem("c_assq"), sem("c_an_ok"), sem("c_at_mm"), sem("c_athi_ok"), sem("c_at_ok")
        y_mm, x1_ok, ssq2, xn2_ok = sem("c_y_mm"), sem("c_x1_ok"), sem("c_ssq2"), sem("c_xn2_ok")
        x1_st, xn_st = [sem(f"c_x1_st{i}") for i in range(2)], [sem(f"c_xn_st{i}") for i in range(2)]
        h2_mm, h2_ok, lg_mm, sel_ok, pos_mm, slot_ok = (sem("c_" + n) for n in (
            "h2_mm", "h2_ok", "lg_mm", "sel_ok", "pos_mm", "slot_ok"))
        list_st = [sem(f"c_list_st{i}") for i in range(2)]
        cnt_mm, dve_own = sem("c_cnt_mm"), sem("c_dve_own")
        tope_ok, ars_ok, xrs_ok, gated = sem("c_tope_ok"), sem("c_ars_ok"), sem("c_xrs_ok"), sem("c_gated")
        an_own, xn_own, choose_own, place_own = sem("c_an_own"), sem("c_xn_own"), sem("c_choose_own"), sem("c_place_own")
        CHOOSE, PLACE = 6, 5

        def steps(eng, step):
            for t in range(-1, 3):
                step(t, t % 2)
            with eng.Fori(0, (NT - 4) // 2) as q:
                step(2 * q + 3, 1)
                step(2 * q + 4, 0)
            for t in range(NT - 1, NT + 3):
                step(t, t % 2)

        def there(t):
            return not isinstance(t, int) or 0 <= t < NT

        def past(t, n):
            return not isinstance(t, int) or t >= n

        with nc.Block() as block:
            @block.sync
            def _(sp):
                for dst, src in ((n2w[:, :], a["norm2_w"].rearrange("a (k p) -> p (a k)", p=P)),
                                 (awbc[:, :], a["attn_out_norm_w"].broadcast_to([P, s.DA])),
                                 (brbc[:, :], a["b_router"].broadcast_to([P, E])),
                                 (wr[:, :, :], a["w_router"][0].rearrange("(k p) e -> p k e", p=P))):
                    sp.dma_start(dst, src).then_inc(small_in, 16)
                for j in range(1, NS):
                    sp.wait_ge(wlo_ok, NP * j)
                    sp.dma_start(wraw[:, :, :], a["w_out"][0].rearrange("(k p) n -> p k n", p=P)
                                 [:, :, j * SL:(j + 1) * SL]).then_inc(w_in, 16)

                def step(t, b):
                    i, b = t + 1, 1 - b
                    if not there(i):
                        return
                    if past(i, 2):
                        sp.wait_ge(xn2_ok, i - 1)
                        s.settle(sp)
                        sp.wait_ge(x1_st[b], 8 * (i - b))
                    sp.dma_start(xt[b][:, :], a["x"][0, bass.ds(i * P, P), :]).then_inc(x_in[b], 16)

                steps(sp, step)
                sp.wait_ge(wlo_ok, NP * NS)
                for h in range(2):
                    sp.dma_start(s.slab[:, :, h * s.GB:(h + 1) * s.GB],
                                 a["w_gate_up"][0, 0].rearrange("(k p) (h n) -> p k h n", p=P, h=2)[:, :, h, 0:s.GB]
                                 ).then_inc(slab_in, 16)
                sp.wait_ge(slab_in, 32)

            @block.gpsimd
            def _(pool):
                own = Chain(pool, pool_own)
                ones32, tri32 = dump[:, 0:P], dump[:, P:2 * P]
                own.link(nc.gpsimd.memset(dump[:, 0:2 * P], 1.0))
                own.link(nc.gpsimd.affine_select(out=tri32, in_=tri32, compare_op=ALU.is_gt, fill=0.0, base=0,
                                                 pattern=[[1, P]], channel_multiplier=-1))
                own.link(nc.gpsimd.tensor_copy(tri[:, :], tri32))
                own.link(nc.gpsimd.tensor_copy(ones_bf[:, :], ones32))
                own.link(nc.gpsimd.memset(sel_before[:, :], 0.0))
                own.link(nc.gpsimd.iota(hotpos[:, 0, :].bitcast(I32), pattern=[[1, E]], base=0, channel_multiplier=0))
                own.link(nc.gpsimd.tensor_copy(iota_e[:, :], hotpos[:, 0, :].bitcast(I32)))
                own.link(nc.gpsimd.iota(hotpos[:, 1, 0:NT].bitcast(I32), pattern=[[P, NT]], base=0, channel_multiplier=1))
                own.link(nc.gpsimd.tensor_copy(tokf[:, :], hotpos[:, 1, 0:NT].bitcast(I32)))
                pool.sem_inc(consts, 1)

                def step(t, b):
                    i, b = t - 3, 1 - b
                    if not there(i):
                        return
                    pool.wait_ge(slot_ok, i + 1)
                    s.settle(pool)
                    for r in range(K4):
                        pool.indirect_dma_start(
                            out=s.list_d[:, :], out_offset=bass.IndirectOffsetOnAxis(ap=slot[b][r][:, :], axis=0),
                            in_=entry[b][r][:, :], in_offset=None).then_inc(list_st[b], 16)

                steps(pool, step)
                for b in range(2):
                    pool.wait_ge(list_st[b], 16 * K4 * NT // 2)

            @block.scalar
            def _(act):
                def split(j):
                    if j:
                        act.wait_ge(w_in, 16 * j)
                    for q in range(NP):
                        part = slice(PIECE * q, PIECE * (q + 1))
                        nc.scalar.activation(whi[j][:, part, :], wraw[:, part, :], ACT.Copy).then_inc(whi_ok, 1)

                split(0)
                for g, dst in enumerate((gate1, s.gate2)):
                    act.wait_ge(bc_mm, g + 1)
                    nc.scalar.activation(dst[:, :], psum[:, 2 * g:2 * g + 2, :].rearrange("p b n -> p (b n)"),
                                         ACT.Copy).then_inc(bc_ok, 1)
                split(1)

                def mean_square(i, b):
                    if past(i, 1):
                        act.wait_ge(assq, i)
                    nc.scalar.activation(adump[:, :], s.attn[:, bass.ds(i, 1), :].rearrange("p a n -> p (a n)"),
                                         ACT.Square, accum_out=st[b][:, 0:1]).then_inc(assq, 1)
                    act.wait_ge(assq, i + 1)
                    nc.scalar.activation(st[b][:, 1:2], st[b][:, 0:1], ACT.Sqrt, bias=s.eps[:, :],
                                         scale=1.0 / s.DA).then_inc(ars_ok, 1)
                    nc.scalar.activation(cthi[b][:, :, :], s.convn[:, :, bass.ds(i * P, P)], ACT.Copy).then_inc(athi_ok, 1)

                def attention_hi(i, b):
                    act.wait_ge(at_mm, i + 1)
                    nc.scalar.activation(athi[b][:, :], psum[:, 4, :], ACT.Copy).then_inc(athi_ok, 1)

                def h2(i, b):
                    act.wait_ge(xn2_ok, i + 1)
                    act.dma_start(s.xn_d[bass.ds(i * P, P), :], xn2[b][:, :]).then_inc(xn_st[b], 16)
                    act.wait_ge(h2_mm, i + 1)
                    for k in range(KT):
                        nc.scalar.activation(h2T[b][:, k, :], psum[:, 5 + k // 4, (k % 4) * P:(k % 4 + 1) * P],
                                             ACT.Identity, bias=s.shift2[:, k:k + 1],
                                             scale=s.gain2[:, k:k + 1]).then_inc(h2_ok, 1)

                def x1_square(i, b):
                    act.wait_ge(x1_ok, i + 1)
                    act.dma_start(s.x1_d[bass.ds(i * P, P), :], xt[b][:, :]).then_inc(x1_st[b], 16)
                    if past(i, 1):
                        act.wait_ge(ssq2, i)
                    nc.scalar.activation(dump[:, :], xt[b][:, :], ACT.Square, accum_out=st[b][:, 3:4]).then_inc(ssq2, 1)
                    act.wait_ge(ssq2, i + 1)
                    nc.scalar.activation(st[b][:, 4:5], st[b][:, 3:4], ACT.Sqrt, bias=s.eps[:, :],
                                         scale=1.0 / D).then_inc(xrs_ok, 1)

                def step(t, b):
                    if there(t + 1):
                        mean_square(t + 1, 1 - b)
                        attention_hi(t + 1, 1 - b)
                    if there(t - 1):
                        h2(t - 1, 1 - b)
                    if there(t):
                        x1_square(t, b)

                act.wait_ge(cols_ok, 2)
                act.wait_ge(consts, 1)
                steps(act, step)
                act.wait_ge(slot_ok, NT)
                nc.scalar.activation(s.topw_all[:, :, :], s.topw_all[:, :, :], ACT.Exp).then_inc(tope_ok, 1)
                for b in range(2):
                    act.wait_ge(x1_st[b], 16 * NT // 2)
                    act.wait_ge(xn_st[b], 16 * NT // 2)

            @block.vector
            def _(dve):
                for j in range(NS):
                    for q in range(NP):
                        part = slice(PIECE * q, PIECE * (q + 1))
                        dve.wait_ge(whi_ok, NP * j + q + 1)
                        nc.vector.tensor_tensor(wlo[j][:, part, :], wraw[:, part, :],
                                                whi[j][:, part, :].bitcast(F32), ALU.subtract).then_inc(wlo_ok, 1)
                    if j == 0:
                        dve.wait_ge(small_in, 16 * 4)
                        dve.wait_ge(consts, 1)
                        dve.wait_ge(cols_mm, 1)
                        nc.vector.tensor_copy(s.shift2[:, :], psum[:, 7, 0:KT]).then_inc(cols_ok, 1)
                        nc.vector.scalar_tensor_tensor(s.gain2[:, :], psum[:, 7, KT:2 * KT], 1.0, n2w[:, :],
                                                       ALU.add, ALU.mult).then_inc(cols_ok, 1)
                dve.wait_ge(bc_ok, 2)

                def attention_norm(i, b):
                    row = st[b]
                    own = Chain(dve, an_own, i)
                    dve.wait_ge(ars_ok, i + 1)
                    own.link(nc.vector.reciprocal(row[:, 2:3], row[:, 1:2]))
                    nc.vector.scalar_tensor_tensor(an[b][:, :], s.attn[:, bass.ds(i, 1), :].rearrange("p a n -> p (a n)"),
                                                   row[:, 2:3], awbc[:, :], ALU.mult, ALU.mult).then_inc(an_ok, 1)
                    dve.wait_ge(athi_ok, 2 * i + 1)
                    nc.vector.tensor_tensor(ctlo[b][:, :, :], s.convn[:, :, bass.ds(i * P, P)],
                                            cthi[b][:, :, :].bitcast(F32), ALU.subtract).then_inc(at_ok, 1)

                def attention_lo(i, b):
                    dve.wait_ge(athi_ok, 2 * i + 2)
                    nc.vector.tensor_tensor(atlo[b][:, :], psum[:, 4, :], athi[b][:, :].bitcast(F32),
                                            ALU.subtract).then_inc(at_ok, 1)

                def residual(i, b):
                    dve.wait_ge(y_mm, i + 1)
                    if past(i, 2):
                        dve.wait_ge(xn_st[b], 8 * (i - b))
                    y = psum[:, 2 * b:2 * b + 2, :].rearrange("p b n -> p (b n)")
                    nc.vector.tensor_tensor(xn2[b][:, :], y, gate1[:, :], ALU.mult).then_inc(gated, 1)
                    dve.wait_ge(gated, i + 1)
                    dve.wait_ge(x_in[b], 8 * (i - b) + 16)
                    nc.vector.tensor_tensor(xt[b][:, :], xn2[b][:, :], xt[b][:, :], ALU.add).then_inc(x1_ok, 1)

                def norm2(i, b):
                    row = st[b]
                    own = Chain(dve, xn_own, i)
                    dve.wait_ge(xrs_ok, i + 1)
                    own.link(nc.vector.reciprocal(row[:, 5:6], row[:, 4:5]))
                    nc.vector.tensor_scalar(xn2[b][:, :], xt[b][:, :], row[:, 5:6], None, ALU.mult).then_inc(xn2_ok, 1)

                def choose(i, b):
                    own = Chain(dve, choose_own, CHOOSE * i)
                    dve.wait_ge(lg_mm, i + 1)
                    own.link(nc.vector.tensor_tensor(lg[:, :], psum[:, 7, 0:E], brbc[:, :], ALU.add))
                    s.settle(dve)
                    own.link(nc.vector.max(top[:, :], lg[:, :]))
                    s.settle(dve)
                    own.link(nc.vector.max_index(topi[:, :], top[:, :], lg[:, :]))
                    own.link(nc.vector.tensor_copy(topf[:, :], topi[:, 0:K4]))
                    nc.vector.tensor_scalar(s.topw_all[:, bass.ds(i, 1), :].rearrange("p a r -> p (a r)"),
                                            top[:, 0:K4], top[:, 0:1], None, ALU.subtract)
                    for r in range(K4):
                        ins = nc.vector.tensor_scalar(hot[:, r, :], iota_e[:, :], topf[:, r:r + 1], None, ALU.is_equal)
                    own.link(ins)
                    nc.vector.tensor_tensor(hotpos[:, 0, :], hot[:, 0, :], hot[:, 1, :], ALU.add)
                    own.link(nc.vector.tensor_tensor(hotpos[:, 1, :], hot[:, 2, :], hot[:, 3, :], ALU.add))
                    nc.vector.tensor_tensor(sel[b][:, :], hotpos[:, 0, :], hotpos[:, 1, :], ALU.add).then_inc(sel_ok, 1)
                    assert own.n == CHOOSE

                def place(i, b):
                    own = Chain(dve, place_own, PLACE * i)
                    dve.wait_ge(pos_mm, i + 1)
                    own.link(nc.vector.tensor_copy(pos[:, :], psum[:, 7, 64:64 + E]))
                    nc.vector.tensor_tensor(sel_before[:, :], sel_before[:, :], sel[b][:, :], ALU.add)
                    own.link(nc.vector.tensor_tensor(hotpos[:, :, :], hot[:, :, :],
                                                     pos[:, :].rearrange("p (a e) -> p a e", a=1).broadcast_to([P, K4, E]),
                                                     ALU.mult))
                    own.link(nc.vector.tensor_reduce(slotf[:, 0:K4], hotpos[:, :, :], AX_X, ALU.add))
                    own.link(nc.vector.scalar_tensor_tensor(slotf[:, K4:2 * K4], topf[:, :], float(T), slotf[:, 0:K4],
                                                            ALU.mult, ALU.add))
                    if not isinstance(i, int):
                        s.settle(dve)
                        with dve.If(i > 1):
                            dve.wait_ge(list_st[b], 8 * K4 * (i - b))
                            s.settle(dve)
                    elif i > 1:
                        dve.wait_ge(list_st[b], 8 * K4 * (i - b))
                        s.settle(dve)
                    for r in range(K4):
                        nc.vector.tensor_copy(slot[b][r][:, :], slotf[:, K4 + r:K4 + r + 1])
                        nc.vector.tensor_copy(entry[b][r][:, 0:1], tokf[:, bass.ds(i, 1)])
                        ins = nc.vector.tensor_scalar(entry[b][r][:, 1:2], tokf[:, bass.ds(i, 1)], float(K4), float(r),
                                                      ALU.mult, ALU.add)
                    own.link(ins)
                    dve.sem_inc(slot_ok, 1)
                    assert own.n == PLACE

                def step(t, b):
                    if there(t + 1):
                        attention_norm(t + 1, 1 - b)
                        attention_lo(t + 1, 1 - b)
                    if there(t):
                        residual(t, b)
                    if there(t - 3):
                        place(t - 3, 1 - b)
                    if there(t - 2):
                        choose(t - 2, b)
                    if there(t):
                        norm2(t, b)

                steps(dve, step)
                own = Chain(dve, dve_own)
                dve.wait_ge(tope_ok, 1)
                own.link(nc.vector.tensor_reduce(topsum[:, 0:NT], s.topw_all[:, :, :], AX_X, ALU.add))
                own.link(nc.vector.reciprocal(topsum[:, NT:2 * NT], topsum[:, 0:NT]))
                own.link(nc.vector.tensor_tensor(s.topw_all[:, :, :], s.topw_all[:, :, :],
                                                 topsum[:, NT:2 * NT].rearrange("p (t a) -> p t a", a=1)
                                                 .broadcast_to([P, NT, K4]), ALU.mult))
                dve.wait_ge(cnt_mm, 1)
                n, more, groups, ends, ones_e = (cnt[:, k * E:(k + 1) * E] for k in range(5))
                own.link(nc.vector.tensor_copy(n, psum[0:1, 7, 0:E]))
                own.link(nc.vector.memset(groups, 1.0))
                own.link(nc.vector.memset(ones_e, 1.0))
                for g in range(1, T // s.GB):
                    own.link(nc.vector.tensor_scalar(more, n, float(g * s.GB), None, ALU.is_gt))
                    own.link(nc.vector.tensor_tensor(groups, groups, more, ALU.add))
                own.link(nc.vector.tensor_tensor_scan(ends, ones_e, groups, 0.0, ALU.mult, ALU.add))
                own.link(nc.vector.memset(s.table[:, :, :], 0))
                own.link(nc.vector.tensor_copy(s.table[:, 0, 1:E + 1], ends))
                own.link(nc.vector.tensor_copy(s.table[:, 1, 0:E], n))

            @block.tensor
            def _(pe):
                for g, at in enumerate((0, 3 * D)):
                    for h in range(2):
                        mm = nc.tensor.matmul(psum[:, 2 * g + h, :], s.ones_row[:, :],
                                              s.modrow[:, at + h * 512:at + (h + 1) * 512], start=True, stop=True)
                    mm.then_inc(bc_mm, 1)
                for k in range(2 * KT):
                    mm = nc.tensor.matmul(psum[:, 7, k:k + 1], s.modrow[:, D + k * P:D + (k + 1) * P],
                                          s.ones_row[:, 0:1], start=True, stop=True)
                mm.then_inc(cols_mm, 1)
                pe.wait_ge(wlo_ok, NS * NP)
                pe.wait_ge(bc_ok, 2)
                pe.wait_ge(cols_ok, 2)

                def turn_attention(i, b):
                    pe.wait_ge(an_ok, i + 1)
                    if past(i, 1):
                        pe.wait_ge(at_ok, 2 * i)
                    for t in range(CT):
                        mm = nc.tensor.transpose(psum[:, 4, t * P:(t + 1) * P], an[b][:, t * P:(t + 1) * P], s.ident[:, :])
                    mm.then_inc(at_mm, 1)

                def project(i, b):
                    pe.wait_ge(at_ok, 2 * i + 2)
                    if past(i, 2):
                        pe.wait_ge(x1_ok, i - 1)
                    for j in range(NS):
                        for kt in range(KT):
                            k = kt % CT
                            hi = athi[b][:, k * P:(k + 1) * P] if kt < CT else cthi[b][:, k, :]
                            lo = atlo[b][:, k * P:(k + 1) * P] if kt < CT else ctlo[b][:, k, :]
                            for q, (m_, w_) in enumerate(((hi, whi), (hi, wlo), (lo, whi))):
                                mm = nc.tensor.matmul(psum[:, 2 * b + j, :], m_, w_[j][:, kt, :],
                                                      start=(kt == 0 and q == 0), stop=(kt == KT - 1 and q == 2))
                    mm.then_inc(y_mm, 1)

                def turn_norm(i, b):
                    pe.wait_ge(xn2_ok, i + 1)
                    if past(i, 1):
                        pe.wait_ge(h2_ok, KT * i)
                    for k in range(KT):
                        mm = nc.tensor.transpose(psum[:, 5 + k // 4, (k % 4) * P:(k % 4 + 1) * P],
                                                 xn2[b][:, k * P:(k + 1) * P], s.ident[:, :])
                    mm.then_inc(h2_mm, 1)

                def logits(i, b):
                    pe.wait_ge(h2_ok, KT * i + KT)
                    if past(i, 1):
                        pe.wait_ge(sel_ok, i)
                    for k in range(KT):
                        mm = nc.tensor.matmul(psum[:, 7, 0:E], h2T[b][:, k, :], wr[:, k, :],
                                              start=(k == 0), stop=(k == KT - 1))
                    mm.then_inc(lg_mm, 1)

                def positions(i, b):
                    pe.wait_ge(sel_ok, i + 1)
                    nc.tensor.matmul(psum[:, 7, 64:64 + E], tri[:, :], sel[b][:, :], start=True, stop=False)
                    nc.tensor.matmul(psum[:, 7, 64:64 + E], ones_bf[:, :], sel_before[:, :],
                                     start=False, stop=True).then_inc(pos_mm, 1)

                def step(t, b):
                    if there(t):
                        project(t, b)
                    if there(t + 1):
                        turn_attention(t + 1, 1 - b)
                    if there(t - 1):
                        turn_norm(t - 1, 1 - b)
                    if there(t - 2):
                        logits(t - 2, b)
                    if there(t - 3):
                        positions(t - 3, 1 - b)

                pe.wait_ge(consts, 1)
                pe.wait_ge(small_in, 16 * 4)
                steps(pe, step)
                pe.wait_ge(slot_ok, NT)
                nc.tensor.matmul(psum[:, 7, 0:E], ones_bf[:, :], sel_before[:, :], start=True,
                                 stop=True).then_inc(cnt_mm, 1)


def expert_block(nc, s, a):
    T, D, KT, E = s.T, s.D, s.KT, s.E
    psum = s.psum
    F = a["w_down"].shape[2]
    SL, HS, GB = 512, 256, s.GB
    GU, DN = 2 * F // SL, D // SL
    SLABS = GU + DN
    NRAW = 3
    PIECE = 2
    NP = KT // PIECE
    LIMIT, ALPHA = 7.0, 1.702
    assert SLABS % NRAW == 0 and SLABS % 2 == 0 and F == D

    with ExitStack() as ctx:
        def sb(name, shape, dt):
            return ctx.enter_context(nc.sbuf_tensor(name, shape, dt))

        sem = s.semaphores(nc)
        raw = [s.slab] + [sb(f"d_raw{i}", [P, KT, SL], F32) for i in range(1, NRAW)]
        whi = [sb(f"d_whi{i}", [P, KT, SL], F32R) for i in range(2)]
        wlo = [sb(f"d_wlo{i}", [P, KT, SL], F32R) for i in range(2)]
        xg = [sb(f"d_xg{b}", [P, D], F32) for b in range(2)]
        entry = [sb(f"d_entry{b}", [P, 2], I32) for b in range(2)]
        ydst = [sb(f"d_ydst{b}", [P, 1], I32) for b in range(2)]
        two = sb("d_two", [1, 1], I32)
        spare = sb("d_spare", [P, 1], F32)
        h32 = sb("d_h32", [P, KT, P], F32)
        xthi = [sb(f"d_xthi{b}", [P, KT, P], F32R) for b in range(2)]
        xtlo = [sb(f"d_xtlo{b}", [P, KT, P], F32R) for b in range(2)]
        athi = [sb(f"d_athi{b}", [P, KT, P], F32R) for b in range(2)]
        atlo = [sb(f"d_atlo{b}", [P, KT, P], F32R) for b in range(2)]
        gate = [sb(f"d_gate{b}", [P, HS], F32) for b in range(2)]
        up = [sb(f"d_up{b}", [P, HS], F32) for b in range(2)]
        sg = [sb(f"d_sg{b}", [P, HS], F32) for b in range(2)]
        prod = [sb(f"d_prod{b}", [P, HS], F32) for b in range(2)]
        yst = [sb(f"d_yst{b}", [P, D], F32) for b in range(2)]
        braw = sb("d_braw", [2 * E, 2 * F + D], F32)
        bhl = sb("d_bhl", [2 * E, 2 * F + D], F32R)
        rowe = sb("d_rowe", [2 * E, P], F32)
        rowi = sb("d_rowi", [2 * E, P], I32)
        colf, coli = sb("d_colf", [2 * E, E], F32), sb("d_coli", [2 * E, E], I32)
        pick = sb("d_pick", [2 * E, P], F32R)

        raw_in = [sem(f"d_raw_in{i}") for i in range(NRAW)]
        b_in, consts, pool_own = sem("d_b_in"), sem("d_consts"), sem("d_pool_own")
        bhi_ok, bhl_ok, pick_ok = sem("d_bhi_ok"), sem("d_bhl_ok"), sem("d_pick_ok")
        entry_in = [sem(f"d_entry_in{b}") for b in range(2)]
        xg_in = [sem(f"d_xg_in{b}") for b in range(2)]
        whi_ok, wlo_ok, wlp_ok = sem("d_whi_ok"), sem("d_wlo_ok"), sem("d_wlp_ok")
        xt_mm = [sem(f"d_xt_mm{b}") for b in range(2)]
        h32_ok = [sem(f"d_h32_ok{b}") for b in range(2)]
        xthi_ok = [sem(f"d_xthi_ok{b}") for b in range(2)]
        xt_ok = [sem(f"d_xt_ok{b}") for b in range(2)]
        gu_mm, gate_ok, up_ok, sg_ok, prod_ok, act_ok = (sem("d_" + n) for n in (
            "gu_mm", "gate_ok", "up_ok", "sg_ok", "prod_ok", "act_ok"))
        at_mm, athi_ok, at_ok, dn_mm, y_ok = (sem("d_" + n) for n in ("at_mm", "athi_ok", "at_ok", "dn_mm", "y_ok"))
        y_st = [sem(f"d_y_st{b}") for b in range(2)]
        CRED = 2 * DN
        POOL_SLABS, HALF = (2,), NP // 2
        own_pieces = [HALF if j in POOL_SLABS else NP for j in range(SLABS)]
        PER_DVE, PER_POOL = sum(own_pieces), HALF * len(POOL_SLABS)

        def split_by_dve(g, j, pieces):
            return PER_DVE * (g + 1) + sum(own_pieces[:j]) + pieces

        def split_by_pool(g, j, pieces):
            return PER_POOL * (g + 1) + HALF * POOL_SLABS.index(j) + pieces

        def groups(eng, body, wants_two=True):
            with eng.Fori(0, E) as e:
                gs = eng.value_load(s.table[0:1, 0, bass.ds(e, 1)], min_val=0, max_val=2 * E)
                ge = eng.value_load(s.table[0:1, 0, bass.ds(e + 1, 1)], min_val=1, max_val=2 * E)
                n = eng.value_load(s.table[0:1, 1, bass.ds(e, 1)], min_val=0, max_val=T)
                with eng.Fori(gs, ge) as g:
                    if not wants_two:
                        body(e, gs, g, 1)
                    else:
                        with eng.If((g - gs) * GB + P < n):
                            body(e, gs, g, 2)
                        with eng.Else():
                            body(e, gs, g, 1)

        def slot_row(eng, e, gs, g, b):
            row = nc.s_assert_within(
                e * T + (g - gs) * GB + b * P, 0, E * T - P,
                skip_runtime_bounds_check_because="an expert has at most T tokens: its groups end within T rows")
            return eng.snap(row)

        def total(eng):
            return eng.value_load(s.table[0:1, 0, E:E + 1], min_val=E, max_val=2 * E)

        def multiplied(eng, g, j):
            if 0 <= j < GU:
                eng.wait_ge(gu_mm, 2 * GU * g + 2 * (j + 1))
            elif j >= GU:
                eng.wait_ge(dn_mm, 2 * DN * g + 2 * (j - GU + 1) + CRED)
            else:
                eng.wait_ge(dn_mm, 2 * DN * g + 2 * (j + DN + 1))

        def arrived(eng, g, j):
            mine = [q for q in range(SLABS) if q % NRAW == j % NRAW]
            per = sum(32 if q < GU else 16 for q in mine)
            upto = sum(32 if q < GU else 16 for q in mine if q <= j)
            eng.wait_ge(raw_in[j % NRAW], per * g + upto)

        with nc.Block() as block:
            @block.sync
            def _(sp):
                gu = a["w_gate_up"][0].rearrange("e (k p) (h n) -> e p k h n", p=P, h=2)
                dn = a["w_down"][0].rearrange("e (k p) n -> e p k n", p=P)

                def load(e, g, j):
                    gb, jb = (g, j - NRAW) if j >= NRAW else (g - 1, j - NRAW + SLABS)
                    sp.wait_ge(wlo_ok, split_by_dve(gb, jb, own_pieces[jb]))
                    if jb in POOL_SLABS:
                        sp.wait_ge(wlp_ok, split_by_pool(gb, jb, HALF))
                    to = raw[j % NRAW]
                    if j < GU:
                        for h in range(2):
                            src = gu[bass.ds(e, 1), :, :, h, j * HS:(j + 1) * HS].rearrange("e p k n -> (e p) k n")
                            sp.dma_start(to[:, :, h * HS:(h + 1) * HS], src).then_inc(raw_in[j % NRAW], 16)
                    else:
                        src = dn[bass.ds(e, 1), :, :, (j - GU) * SL:(j - GU + 1) * SL].rearrange("e p k n -> (e p) k n")
                        sp.dma_start(to[:, :, :], src).then_inc(raw_in[j % NRAW], 16)

                for rows in (slice(0, E), slice(E, 2 * E)):
                    for h in range(2):
                        sp.dma_start(braw[rows, 0:2 * F].rearrange("e (j h n) -> e j h n", h=2, n=HS)[:, :, h, :],
                                     a["b_gate_up"][0].rearrange("e (h j n) -> e j h n", h=2, n=HS)[:, :, h, :]
                                     ).then_inc(b_in, 16)
                sp.dma_start(braw[0:E, 2 * F:], a["b_down"][0]).then_inc(b_in, 16)
                sp.dma_start(braw[E:2 * E, 2 * F:], a["b_down"][0]).then_inc(b_in, 16)

                def body(e, gs, g, blocks):
                    with sp.If(g > 0):
                        load(e, g, 0)
                    for j in range(1, SLABS):
                        load(e, g, j)

                sp.sem_inc(wlo_ok, PER_DVE)
                sp.sem_inc(wlp_ok, PER_POOL)
                sp.sem_inc(raw_in[0], 32)
                sp.wait_ge(xg_in[0], 16)
                groups(sp, body, wants_two=False)
                load(0, total(sp), 0)

            @block.gpsimd
            def _(pool):
                own = Chain(pool, pool_own)
                own.link(nc.gpsimd.iota(rowi[0:E, :], pattern=[[0, P]], base=0, channel_multiplier=1))
                own.link(nc.gpsimd.iota(rowi[E:2 * E, :], pattern=[[0, P]], base=0, channel_multiplier=1))
                own.link(nc.gpsimd.tensor_copy(rowe[:, :], rowi[:, :]))
                own.link(nc.gpsimd.iota(coli[:, :], pattern=[[1, E]], base=0, channel_multiplier=0))
                own.link(nc.gpsimd.tensor_copy(colf[:, :], coli[:, :]))
                pool.sem_inc(consts, 1)

                LINKS = 3
                for b in range(2):
                    own.link(nc.gpsimd.iota(ydst[b][:, :], pattern=[[0, 1]], base=s.TOPK * T, channel_multiplier=1))
                own.link(nc.gpsimd.memset(yst[0][:, :], 0.0))
                own.link(nc.gpsimd.memset(two[:, :], 0))
                start = own.n

                def gather(b, e, gs, g, real):
                    at = slot_row(pool, e, gs, g, b)
                    pool.dma_start(entry[b][:, :], s.list_d[bass.ds(at, P), :]).then_inc(entry_in[b], 16)
                    pool.wait_ge(entry_in[b], 16 * (g + 1))
                    s.settle(pool)
                    if real:
                        pool.indirect_dma_start(out=xg[b][:, :], out_offset=None, in_=s.xn_d[:, :],
                                                in_offset=bass.IndirectOffsetOnAxis(ap=entry[b][:, 0:1], axis=0)
                                                ).then_inc(xg_in[b], 16)
                    else:
                        pool.dma_start(xg[b][:, 0:1], s.xn_d[0:P, 0:1]).then_inc(xg_in[b], 16)

                def store(g):
                    pool.wait_ge(y_ok, CRED + 2 * DN * g)

                    def scatter(b):
                        pool.indirect_dma_start(out=s.y_d[:, :],
                                                out_offset=bass.IndirectOffsetOnAxis(ap=ydst[b][:, :], axis=0),
                                                in_=yst[b][:, :], in_offset=None).then_inc(y_st[b], 16)

                    s.settle(pool)
                    scatter(0)
                    has_two = pool.value_load(two[0:1, 0:1], min_val=0, max_val=1)
                    with pool.If(has_two > 0):
                        scatter(1)
                    with pool.Else():
                        pool.dma_start(spare[:, :], s.xn_d[0:P, 0:1]).then_inc(y_st[1], 16)
                    for b in range(2):
                        pool.wait_ge(y_st[b], 16 * (g + 1))
                    s.settle(pool)

                def body(e, gs, g, blocks):
                    own = Chain(pool, pool_own, start + LINKS * g)
                    gather(0, e, gs, g, True)
                    gather(1, e, gs, g, blocks == 2)
                    store(g)
                    for b in range(2):
                        own.link(nc.gpsimd.tensor_copy(ydst[b][:, :], entry[b][:, 1:2]))
                        s.settle(pool)
                    own.link(nc.gpsimd.memset(two[:, :], blocks - 1))
                    for b in range(2):
                        pool.wait_ge(xg_in[b], 16 * (g + 1))
                        pool.wait_ge(xt_mm[b], g + 1)
                        s.settle(pool)
                    for j in POOL_SLABS:
                        for q in range(HALF, NP):
                            part = slice(PIECE * q, PIECE * (q + 1))
                            pool.wait_ge(whi_ok, NP * (SLABS * g + j) + q + 1)
                            nc.gpsimd.tensor_tensor(wlo[j % 2][:, part, :], raw[j % NRAW][:, part, :],
                                                    whi[j % 2][:, part, :].bitcast(F32), ALU.subtract).then_inc(wlp_ok, 1)

                groups(pool, body)
                g = total(pool)
                pool.indirect_dma_start(out=xg[0][:, :], out_offset=None, in_=s.xn_d[:, :],
                                        in_offset=bass.IndirectOffsetOnAxis(ap=entry[0][:, 0:1], axis=0)
                                        ).then_inc(xg_in[0], 16)
                store(g)
                pool.wait_ge(xg_in[0], 16 * g + 16)
                s.settle(pool)

            @block.scalar
            def _(act):
                nc.scalar.activation(sg[0][:, 0:1], s.eps[:, :], ACT.Sigmoid).then_inc(bhi_ok, 1)
                act.wait_ge(b_in, 16 * 6)
                nc.scalar.activation(bhl[:, :], braw[:, :], ACT.Copy).then_inc(bhi_ok, 1)
                act.sem_inc(y_ok, CRED)

                def split(g, j, pieces):
                    if 0 in pieces:
                        arrived(act, g, j) if j < SLABS else arrived(act, g + 1, 0)
                        multiplied(act, g, j - 2)
                    for q in pieces:
                        part = slice(PIECE * q, PIECE * (q + 1))
                        nc.scalar.activation(whi[j % 2][:, part, :], raw[j % NRAW][:, part, :],
                                             ACT.Copy).then_inc(whi_ok, 1)

                def xt(b, count):
                    act.wait_ge(xt_mm[b], count)
                    for k in range(KT):
                        nc.scalar.activation(h32[:, k, :], psum[:, 6 + k // 4, (k % 4) * P:(k % 4 + 1) * P],
                                             ACT.Identity, bias=s.shift2[:, k:k + 1],
                                             scale=s.gain2[:, k:k + 1]).then_inc(h32_ok[b], 1)
                    act.wait_ge(h32_ok[b], KT * count)
                    nc.scalar.activation(xthi[b][:, :, :], h32[:, :, :], ACT.Copy).then_inc(xthi_ok[b], 1)

                def sigmoid(g, j, b, sh):
                    act.wait_ge(gate_ok, 2 * GU * g + 2 * j + (b + 1) * sh)
                    nc.scalar.activation(sg[b][:, :], gate[b][:, :], ACT.Sigmoid, scale=ALPHA).then_inc(sg_ok, sh)

                def output(g, jd, b, sh):
                    act.wait_ge(dn_mm, CRED + 2 * DN * g + 2 * jd + (b + 1) * sh)
                    act.wait_ge(y_st[b], 16 * (g + 1))
                    nc.scalar.activation(yst[b][:, jd * SL:(jd + 1) * SL], psum[:, 2 * ((GU + jd) % 2) + b, :],
                                         ACT.Copy).then_inc(y_ok, sh)

                def turned(g, j, b, sh):
                    act.wait_ge(at_mm, 2 * GU * g + 2 * j + (b + 1) * sh)
                    o = (j % 2) * HS
                    nc.scalar.activation(athi[b][:, 2 * j:2 * j + 2, :].rearrange("p k n -> p (k n)"),
                                         psum[:, 4 + b, o:o + HS], ACT.Copy).then_inc(athi_ok, sh)

                def body(e, gs, g, blocks):
                    sh = 2 // blocks
                    if blocks == 2:
                        act.wait_ge(xt_ok[0], g + 1)
                        xt(1, g + 1)
                    else:
                        act.sem_inc(h32_ok[1], KT)
                        act.sem_inc(xthi_ok[1], 1)
                    for j in range(SLABS):
                        before = 1 <= j <= GU
                        split(g, j + 1, [0])
                        for b in range(blocks):
                            if before:
                                sigmoid(g, j - 1, b, sh)
                        split(g, j + 1, [1])
                        if j == SLABS - 1:
                            act.wait_ge(xt_ok[1], g + 1)
                            xt(0, g + 2)
                        if j < GU:
                            split(g, j + 1, [2])
                        for b in range(blocks):
                            if before:
                                turned(g, j - 1, b, sh)
                            elif j > GU:
                                output(g, j - 1 - GU, b, sh)
                        split(g, j + 1, [3] if j < GU else [2, 3])
                    for b in range(blocks):
                        output(g, DN - 1, b, sh)

                xt(0, 1)
                split(0, 0, range(NP))
                groups(act, body)

            @block.vector
            def _(dve):
                lower = slice(E, 2 * E)
                dve.wait_ge(bhi_ok, 2)
                nc.vector.tensor_tensor(bhl[lower, :], braw[lower, :], bhl[lower, :].bitcast(F32),
                                        ALU.subtract).then_inc(bhl_ok, 1)
                dve.wait_ge(consts, 1)

                def xt_low(b, count):
                    dve.wait_ge(xthi_ok[b], count)
                    nc.vector.tensor_tensor(xtlo[b][:, :, :], h32[:, :, :], xthi[b][:, :, :].bitcast(F32),
                                            ALU.subtract).then_inc(xt_ok[b], 1)

                def split(g, j, pieces):
                    for q in pieces:
                        if q >= own_pieces[j % SLABS]:
                            continue
                        part = slice(PIECE * q, PIECE * (q + 1))
                        dve.wait_ge(whi_ok, NP * (SLABS * g + j) + q + 1)
                        nc.vector.tensor_tensor(wlo[j % 2][:, part, :], raw[j % NRAW][:, part, :],
                                                whi[j % 2][:, part, :].bitcast(F32), ALU.subtract).then_inc(wlo_ok, 1)

                def turned(g, j, b, sh):
                    dve.wait_ge(athi_ok, 2 * GU * g + 2 * j + (b + 1) * sh)
                    o = (j % 2) * HS
                    nc.vector.tensor_tensor(atlo[b][:, 2 * j:2 * j + 2, :].rearrange("p k n -> p (k n)"),
                                            psum[:, 4 + b, o:o + HS],
                                            athi[b][:, 2 * j:2 * j + 2, :].rearrange("p k n -> p (k n)").bitcast(F32),
                                            ALU.subtract).then_inc(at_ok, sh)

                def swiglu(g, j, b, sh):
                    count = 2 * GU * g + 2 * j + (b + 1) * sh
                    src = psum[:, 2 * (j % 2) + b, :]
                    dve.wait_ge(gu_mm, count)
                    nc.vector.tensor_scalar(gate[b][:, :], src[:, 0:HS], LIMIT, None, ALU.min).then_inc(gate_ok, sh)
                    nc.vector.tensor_scalar(up[b][:, :], src[:, HS:SL], LIMIT, -LIMIT,
                                            ALU.min, ALU.max).then_inc(up_ok, sh)
                    dve.wait_ge(up_ok, count)
                    dve.wait_ge(gate_ok, count)
                    nc.vector.scalar_tensor_tensor(prod[b][:, :], up[b][:, :], 1.0, gate[b][:, :],
                                                   ALU.add, ALU.mult).then_inc(prod_ok, sh)

                def times_sigmoid(g, j, b, sh):
                    count = 2 * GU * g + 2 * j + (b + 1) * sh
                    dve.wait_ge(prod_ok, count)
                    dve.wait_ge(sg_ok, count)
                    nc.vector.tensor_tensor(up[b][:, :], prod[b][:, :], sg[b][:, :], ALU.mult).then_inc(act_ok, sh)

                def body(e, gs, g, blocks):
                    sh = 2 // blocks
                    def choose_bias():
                        multiplied(dve, g, -1)
                        nc.vector.tensor_scalar(pick[:, :], rowe[:, :], colf[:, bass.ds(e, 1)], None,
                                                ALU.is_equal).then_inc(pick_ok, 1)

                    if blocks == 2:
                        choose_bias()
                        xt_low(1, g + 1)
                    else:
                        dve.sem_inc(xt_ok[1], 1)
                    for j in range(SLABS):
                        before = 1 <= j <= GU
                        for b in range(blocks):
                            if before:
                                swiglu(g, j - 1, b, sh)
                        split(g, j + 1, [0])
                        if j == 0 and blocks == 1:
                            choose_bias()
                        for b in range(blocks):
                            if before:
                                times_sigmoid(g, j - 1, b, sh)
                        split(g, j + 1, [1])
                        if j == SLABS - 1:
                            xt_low(0, g + 2)
                        if j < GU:
                            split(g, j + 1, [2])
                        for b in range(blocks):
                            if before:
                                turned(g, j - 1, b, sh)
                        split(g, j + 1, [3] if j < GU else [2, 3])

                xt_low(0, 1)
                split(0, 0, range(NP))
                groups(dve, body)

            @block.tensor
            def _(pe):
                pe.sem_inc(dn_mm, CRED)
                pe.wait_ge(bhl_ok, 1)

                def xt(b, count):
                    pe.wait_ge(xg_in[b], 16 * count)
                    for k in range(KT):
                        mm = nc.tensor.transpose(psum[:, 6 + k // 4, (k % 4) * P:(k % 4 + 1) * P],
                                                 xg[b][:, k * P:(k + 1) * P], s.ident[:, :])
                    mm.then_inc(xt_mm[b], 1)

                def turn(g, j, b, sh):
                    pe.wait_ge(act_ok, 2 * GU * g + 2 * j + (b + 1) * sh)
                    if j >= 2:
                        pe.wait_ge(at_ok, 2 * GU * g + 2 * (j - 2) + (b + 1) * sh)
                    for t in range(2):
                        o = (j % 2) * HS + t * P
                        mm = nc.tensor.transpose(psum[:, 4 + b, o:o + P], up[b][:, t * P:(t + 1) * P], s.ident[:, :])
                    mm.then_inc(at_mm, sh)

                def unit(g, j, b, sh, blocks):
                    w = j % 2
                    to = psum[:, 2 * w + b, :]
                    if j < DN:
                        pe.wait_ge(y_ok, 2 * DN * g + 2 * (j + 1))
                    else:
                        pe.wait_ge(up_ok, 2 * GU * g + 2 * (j - 2) + (b + 1) * sh)
                    if j == 0:
                        pe.wait_ge(xt_ok[b], g + 1)
                    if j == GU:
                        pe.wait_ge(at_ok, 2 * GU * g + 2 * (GU - 2) + (b + 1) * sh)
                    hi, lo = (xthi, xtlo) if j < GU else (athi, atlo)
                    for k in range(KT):
                        if b == 0 and k % PIECE == 0:
                            q = k // PIECE
                            if q < own_pieces[j]:
                                pe.wait_ge(wlo_ok, split_by_dve(g, j, q + 1))
                            else:
                                pe.wait_ge(wlp_ok, split_by_pool(g, j, q + 1 - HALF))
                        if b == 0 and 1 <= j <= GU and k == (KT - 1 if j < GU else KT // 2):
                            for bb in range(blocks):
                                turn(g, j - 1, bb, sh)
                        if j == GU and k == KT - 2:
                            pe.wait_ge(at_ok, 2 * GU * g + 2 * (GU - 1) + (b + 1) * sh)
                        for q, (m_, w_) in enumerate(((hi, whi), (hi, wlo), (lo, whi))):
                            nc.tensor.matmul(to, m_[b][:, k, :], w_[w][:, k, :], start=(k == 0 and q == 0), stop=False)
                    if j == 0 and b == 0:
                        pe.wait_ge(pick_ok, g + 1)
                    at = j * SL if j < GU else 2 * F + (j - GU) * SL
                    mm = nc.tensor.matmul(to, pick[:, :], bhl[:, at:at + SL], start=False, stop=True)
                    return mm

                def body(e, gs, g, blocks):
                    sh = 2 // blocks
                    if blocks == 2:
                        pe.wait_ge(xt_ok[0], g + 1)
                        xt(1, g + 1)
                    else:
                        pe.sem_inc(xt_mm[1], 1)
                    for j in range(SLABS):
                        if j == SLABS - 1:
                            pe.wait_ge(xt_ok[1], g + 1)
                            xt(0, g + 2)
                        for b in range(blocks):
                            mm = unit(g, j, b, sh, blocks)
                            mm.then_inc(gu_mm if j < GU else dn_mm, sh)

                xt(0, 1)
                groups(pe, body)


def combine_block(nc, s, a, out):
    T, D, NT, K4 = s.T, s.D, s.NT, s.TOPK
    with ExitStack() as ctx:
        def sb(name, shape, dt):
            return ctx.enter_context(nc.sbuf_tensor(name, shape, dt))

        sem = s.semaphores(nc)
        y = [sb(f"e_y{i}", [P, K4, D], F32) for i in range(2)]
        x1 = [sb(f"e_x1_{i}", [P, D], F32) for i in range(2)]
        acc = [sb(f"e_acc{i}", [P, D], F32) for i in range(2)]
        acc_ok, own, done = sem("e_acc_ok"), sem("e_own"), sem("e_done")
        y_in = [sem(f"e_y_in{i}") for i in range(2)]
        x1_in, out_st = [sem(f"e_x1_in{i}") for i in range(2)], [sem(f"e_out_st{i}") for i in range(2)]

        def tiles(eng, tile):
            for b in range(2):
                tile(b, b, 0)
            with eng.Fori(1, NT // 2) as q:
                for b in range(2):
                    tile(2 * q + b, b, q)

        with nc.Block() as block:
            @block.sync
            def _(sp):
                def tile(i, b, q):
                    if not isinstance(q, int):
                        sp.wait_ge(done, 2 * q)
                    sp.dma_start(y[b][:, :, :], s.y_d[0:T * K4, :].rearrange("(i p r) d -> i p r d", p=P, r=K4)
                                 [bass.ds(i, 1), :, :, :].rearrange("i p r d -> (i p) r d")).then_inc(y_in[b], 16)
                    if not isinstance(q, int):
                        sp.wait_ge(out_st[b], 16 * q)
                    sp.dma_start(x1[b][:, :], s.x1_d[bass.ds(i * P, P), :]).then_inc(x1_in[b], 16)

                tiles(sp, tile)

            @block.scalar
            def _(act):
                def tile(i, b, q):
                    act.wait_ge(y_in[b], 16 * q + 16)
                    if not isinstance(q, int):
                        act.wait_ge(done, 2 * q)
                    nc.scalar.activation(acc[b][:, :], y[b][:, 0, :], ACT.Copy,
                                         scale=s.topw_all[:, bass.ds(i, 1), 0]).then_inc(acc_ok, 1)
                    act.wait_ge(done, i + 1)
                    act.dma_start(out[0, bass.ds(i * P, P), :], x1[b][:, :]).then_inc(out_st[b], 16)

                tiles(act, tile)
                for b in range(2):
                    act.wait_ge(out_st[b], 16 * NT // 2)

            @block.vector
            def _(dve):
                def tile(i, b, q):
                    chain = Chain(dve, own, 4 * i)
                    dve.wait_ge(acc_ok, i + 1)
                    for r in range(1, K4):
                        chain.link(nc.vector.scalar_tensor_tensor(acc[b][:, :], y[b][:, r, :],
                                                                  s.topw_all[:, bass.ds(i, 1), r], acc[b][:, :],
                                                                  ALU.mult, ALU.add))
                    chain.link(nc.vector.tensor_tensor(acc[b][:, :], acc[b][:, :], s.gate2[:, :], ALU.mult))
                    dve.wait_ge(x1_in[b], 16 * q + 16)
                    nc.vector.tensor_tensor(x1[b][:, :], acc[b][:, :], x1[b][:, :], ALU.add).then_inc(done, 1)

                tiles(dve, tile)


def build(nc, arrays, out):
    with ExitStack() as ctx:
        ctx.enter_context(nc.allow_non_contiguous_dma(reason="vectors of up to 4 KB, turned to columns"))
        s = shared(nc, ctx, arrays)
        s.slab = s.sb("slab", [P, s.KT, s.HALF], F32)
        with ExitStack() as mixer:
            s.convn = s.sb("convn", [P, s.CT, s.T], F32, mixer)
            project_block(nc, s, arrays)
            s.release(nc)
            s.attn = s.sb("attn", [P, s.NT, s.DA], F32, mixer)
            s.modrow = s.sb("modrow", [1, 4 * s.D], F32, mixer)
            attention_block(nc, s, arrays)
            s.release(nc)
            mixer_block(nc, s, arrays)
            s.release(nc)
        expert_block(nc, s, arrays)
        s.release(nc)
        combine_block(nc, s, arrays, out)


_INS = ['x', 'c', 'w_ada', 'b_ada', 'norm1_w', 'w_in', 'b_forget', 'q_norm_w', 'k_norm_w', 'conv_w',
        'attn_out_norm_w', 'conv_out_norm_w', 'w_out', 'norm2_w', 'w_router', 'b_router',
        'w_gate_up', 'b_gate_up', 'w_down', 'b_down']
_OUTS = [((1, 1024, 1024), 'float32')]


def kernel(**inputs):
    import numpy as _np
    import concourse.bacc as _bacc
    from concourse import mybir as _mybir
    from concourse.bass_utils import run_bass_kernel_spmd as _run

    nc = _bacc.Bacc("TRN2", target_bir_lowering=False, num_devices=1)
    arrays, args = {}, {}
    for name in _INS:
        v = _np.ascontiguousarray(inputs[name])
        arrays[f"in_{name}_dram"] = v
        args[name] = nc.dram_tensor(f"in_{name}_dram", v.shape, _mybir.dt.from_np(v.dtype), kind="ExternalInput").ap()
    (shape, dtype), = _OUTS
    out = nc.dram_tensor("out_0_dram", shape, _mybir.dt.from_np(_np.dtype(dtype)), kind="ExternalOutput").ap()
    build(nc, args, out)
    r = _run(nc, [arrays], core_ids=[0])
    return r.results[0]["out_0_dram"]
```
